# Optimizing a Trainium2 kernel written in Bass

```python
import math
import jax, jax.numpy as jnp
from jax import lax
import numpy as np

D_MODEL = 1024
BATCH = 1
SEQ = 512
DEPTH = 2
DEC_BATCH = 8
DEC_SEQ = 1
PAST_LEN = 4096
PAGE_SIZE = 128

N_MIXERS = 2
N_A_LAYERS = (DEPTH + 1) // 2
N_B_LAYERS = DEPTH // 2
D_CONV = D_MODEL
CONV_A_W = 3
D_RNN = D_MODEL
N_RG_BLOCKS = 8
RG_BLOCK = D_RNN // N_RG_BLOCKS
CONV_B_W = 4
RG_C = 8.0
N_GROUPS = 4
EXP_PER_GROUP = 8
N_EXPERTS = N_GROUPS * EXP_PER_GROUP
TOP_K = 2
D_EXPERT = 512
MOE_BLOCK = 128
ALPHA = (2.0 * DEPTH) ** 0.25
BETA = (8.0 * DEPTH) ** -0.25
LN_EPS = 1e-5

kernel_name = "hybrid_shortconv_rglru_hmoe_step"

def layer_norm(x, g, b):
    xf = x.astype(jnp.float32)
    mu = jnp.mean(xf, axis=-1, keepdims=True)
    var = jnp.mean(jnp.square(xf - mu), axis=-1, keepdims=True)
    y = (xf - mu) * lax.rsqrt(var + LN_EPS)
    return (y * g.astype(jnp.float32) + b.astype(jnp.float32)).astype(x.dtype)

def causal_dwconv(u, buf, w):
    width = w.shape[0]
    s = u.shape[1]
    full = jnp.concatenate([buf.astype(u.dtype), u], axis=1)
    out = full[:, 0:s] * w[0]
    for k in range(1, width):
        out = out + full[:, k:k + s] * w[k]
    return out, full[:, s:]

def short_conv_mixer(x, buf, w_in, conv_w, w_out):
    bcx = jnp.einsum('bsd,de->bse', x, w_in)
    gb, gc, xh = jnp.split(bcx, 3, axis=-1)
    conv, new_buf = causal_dwconv(gc * xh, buf, conv_w)
    y = jnp.einsum('bsc,cd->bsd', gb * conv, w_out)
    return y, new_buf

def block_diag(x, w, bias):
    b, s, _ = x.shape
    xb = x.reshape(b, s, N_RG_BLOCKS, RG_BLOCK)
    y = jnp.einsum('bsnk,nkj->bsnj', xb, w).reshape(b, s, D_RNN)
    return y + bias

def rglru(x, h0, ga_w, ga_b, gx_w, gx_b, lam):
    r = jax.nn.sigmoid(block_diag(x, ga_w, ga_b).astype(jnp.float32))
    i = jax.nn.sigmoid(block_diag(x, gx_w, gx_b).astype(jnp.float32))
    log_a = -RG_C * r * jax.nn.softplus(-lam.astype(jnp.float32))
    a = jnp.exp(log_a)
    mult = jnp.sqrt(-jnp.expm1(2.0 * log_a))
    bterm = mult * (i * x.astype(jnp.float32))
    bterm = bterm.at[:, 0].add(a[:, 0] * h0.astype(jnp.float32))

    def combine(left, right):
        a1, b1 = left
        a2, b2 = right
        return a1 * a2, a2 * b1 + b2

    _, h = lax.associative_scan(combine, (a, bterm), axis=1)
    return h.astype(x.dtype), h[:, -1].astype(h0.dtype)

def rglru_mixer(x, conv_buf, h0, w_in, conv_w, conv_b, ga_w, ga_b, gx_w, gx_b, lam, w_out):
    gx = jnp.einsum('bsd,de->bse', x, w_in)
    gate, xr = jnp.split(gx, 2, axis=-1)
    xc, new_buf = causal_dwconv(xr, conv_buf, conv_w)
    xc = xc + conv_b
    h, h_last = rglru(xc, h0, ga_w, ga_b, gx_w, gx_b, lam)
    y = jnp.einsum('bsc,cd->bsd', jax.nn.gelu(gate, approximate=True) * h, w_out)
    return y, new_buf, h_last

def hier_moe(x, w_group, w_expert, w_gate, w_up, w_down):
    bsz, s, d = x.shape
    t = bsz * s
    x2 = x.reshape(t, d)
    gp = jax.nn.softmax((x2 @ w_group).astype(jnp.float32), axis=-1)
    g = jnp.argmax(gp, axis=-1).astype(jnp.int32)
    gw = jnp.max(gp, axis=-1)
    el = (x2 @ w_expert).astype(jnp.float32).reshape(t, N_GROUPS, EXP_PER_GROUP)
    el = jnp.take_along_axis(el, g[:, None, None], axis=1)[:, 0]
    ep = jax.nn.softmax(el, axis=-1)
    vals, idx = lax.top_k(ep, TOP_K)
    vals = vals / jnp.sum(vals, axis=-1, keepdims=True)
    wts = gw[:, None] * vals
    eid = (g[:, None] * EXP_PER_GROUP + idx).reshape(-1).astype(jnp.int32)
    tok = jnp.repeat(jnp.arange(t, dtype=jnp.int32), TOP_K)
    wa = wts.reshape(-1)
    n_assign = t * TOP_K
    order = jnp.argsort(eid)
    eid_s, tok_s, w_s = eid[order], tok[order], wa[order]
    counts = jnp.zeros((N_EXPERTS,), jnp.int32).at[eid].add(1)
    starts = jnp.cumsum(counts) - counts
    pcounts = (counts + MOE_BLOCK - 1) // MOE_BLOCK * MOE_BLOCK
    pend = jnp.cumsum(pcounts)
    pstarts = pend - pcounts
    dest = pstarts[eid_s] + (jnp.arange(n_assign, dtype=jnp.int32) - starts[eid_s])
    n_blk = (n_assign + N_EXPERTS * (MOE_BLOCK - 1) + MOE_BLOCK - 1) // MOE_BLOCK
    p_rows = n_blk * MOE_BLOCK
    row_tok = jnp.full((p_rows,), t, jnp.int32).at[dest].set(tok_s)
    x_pad = jnp.concatenate([x2, jnp.zeros((1, d), x2.dtype)], axis=0)
    xs = x_pad[row_tok].reshape(n_blk, MOE_BLOCK, d)
    blk_e = jnp.clip(jnp.searchsorted(pend, jnp.arange(n_blk, dtype=jnp.int32) * MOE_BLOCK, side='right'),
                     0, N_EXPERTS - 1).astype(jnp.int32)

    def expert_block(args):
        xb, e = args
        hmid = jax.nn.silu(xb @ w_gate[e]) * (xb @ w_up[e])
        return hmid @ w_down[e]

    out = lax.map(expert_block, (xs, blk_e)).reshape(p_rows, d)
    y_rows = out[dest] * w_s[:, None].astype(out.dtype)
    y = jax.ops.segment_sum(y_rows, tok_s, num_segments=t)
    return y.reshape(bsz, s, d)

def setup_inputs(seed: int = 0) -> dict:
    key = jax.random.key(seed)
    ks = iter(jax.random.split(key, 40))
    f32 = jnp.float32

    def nrm(shape, scale):
        return jax.random.normal(next(ks), shape, f32) * scale

    x_prompt = nrm((BATCH, SEQ, D_MODEL), 1.0)
    x_sample = nrm((DEC_BATCH, DEC_SEQ, D_MODEL), 1.0)
    state_conv_a = nrm((N_A_LAYERS, DEC_BATCH, CONV_A_W - 1, D_CONV), 1.0)
    state_conv_b = nrm((N_B_LAYERS, DEC_BATCH, CONV_B_W - 1, D_RNN), 1.0)
    state_h = nrm((N_B_LAYERS, DEC_BATCH, D_RNN), 0.5)
    a_w_in = nrm((N_A_LAYERS, D_MODEL, 3 * D_CONV), D_MODEL ** -0.5)
    a_conv_w = nrm((N_A_LAYERS, CONV_A_W, D_CONV), CONV_A_W ** -0.5)
    a_w_out = nrm((N_A_LAYERS, D_CONV, D_MODEL), D_CONV ** -0.5 * BETA)
    b_w_in = nrm((N_B_LAYERS, D_MODEL, 2 * D_RNN), D_MODEL ** -0.5)
    b_conv_w = nrm((N_B_LAYERS, CONV_B_W, D_RNN), CONV_B_W ** -0.5)
    b_conv_b = nrm((N_B_LAYERS, D_RNN), 0.01)
    b_gate_a_w = nrm((N_B_LAYERS, N_RG_BLOCKS, RG_BLOCK, RG_BLOCK), RG_BLOCK ** -0.5)
    b_gate_a_b = nrm((N_B_LAYERS, D_RNN), 0.01)
    b_gate_x_w = nrm((N_B_LAYERS, N_RG_BLOCKS, RG_BLOCK, RG_BLOCK), RG_BLOCK ** -0.5)
    b_gate_x_b = nrm((N_B_LAYERS, D_RNN), 0.01)
    a_c = jax.random.uniform(next(ks), (N_B_LAYERS, D_RNN), f32, 0.9, 0.999)
    a_base = a_c ** (1.0 / RG_C)
    b_lambda = jnp.log(a_base) - jnp.log1p(-a_base)
    b_w_out = nrm((N_B_LAYERS, D_RNN, D_MODEL), D_RNN ** -0.5 * BETA)
    ln1_g = 1.0 + nrm((DEPTH, D_MODEL), 0.02)
    ln1_b = nrm((DEPTH, D_MODEL), 0.02)
    ln2_g = 1.0 + nrm((DEPTH, D_MODEL), 0.02)
    ln2_b = nrm((DEPTH, D_MODEL), 0.02)
    moe_w_group = nrm((DEPTH, D_MODEL, N_GROUPS), D_MODEL ** -0.5)
    moe_w_expert = nrm((DEPTH, D_MODEL, N_EXPERTS), D_MODEL ** -0.5)
    moe_w_gate = nrm((DEPTH, N_EXPERTS, D_MODEL, D_EXPERT), D_MODEL ** -0.5)
    moe_w_up = nrm((DEPTH, N_EXPERTS, D_MODEL, D_EXPERT), D_MODEL ** -0.5)
    moe_w_down = nrm((DEPTH, N_EXPERTS, D_EXPERT, D_MODEL), D_EXPERT ** -0.5 * BETA)
    return {
        "x_prompt": x_prompt, "x_sample": x_sample,
        "state_conv_a": state_conv_a, "state_conv_b": state_conv_b, "state_h": state_h,
        "a_w_in": a_w_in, "a_conv_w": a_conv_w, "a_w_out": a_w_out,
        "b_w_in": b_w_in, "b_conv_w": b_conv_w, "b_conv_b": b_conv_b,
        "b_gate_a_w": b_gate_a_w, "b_gate_a_b": b_gate_a_b,
        "b_gate_x_w": b_gate_x_w, "b_gate_x_b": b_gate_x_b,
        "b_lambda": b_lambda, "b_w_out": b_w_out,
        "ln1_g": ln1_g, "ln1_b": ln1_b, "ln2_g": ln2_g, "ln2_b": ln2_b,
        "moe_w_group": moe_w_group, "moe_w_expert": moe_w_expert,
        "moe_w_gate": moe_w_gate, "moe_w_up": moe_w_up, "moe_w_down": moe_w_down,
    }

def reference(x_prompt, x_sample, state_conv_a, state_conv_b, state_h,
              a_w_in, a_conv_w, a_w_out,
              b_w_in, b_conv_w, b_conv_b, b_gate_a_w, b_gate_a_b, b_gate_x_w, b_gate_x_b,
              b_lambda, b_w_out,
              ln1_g, ln1_b, ln2_g, ln2_b,
              moe_w_group, moe_w_expert, moe_w_gate, moe_w_up, moe_w_down):
    xp, xs = x_prompt, x_sample
    bp = x_prompt.shape[0]
    conv_a_p, conv_a_s, conv_b_p, conv_b_s, h_p, h_s = [], [], [], [], [], []
    for i in range(DEPTH):
        j = i // N_MIXERS
        if i % N_MIXERS == 0:
            buf0 = jnp.zeros((bp, CONV_A_W - 1, D_CONV), xp.dtype)
            yp, nbp = short_conv_mixer(xp, buf0, a_w_in[j], a_conv_w[j], a_w_out[j])
            ys, nbs = short_conv_mixer(xs, state_conv_a[j], a_w_in[j], a_conv_w[j], a_w_out[j])
            conv_a_p.append(nbp)
            conv_a_s.append(nbs)
        else:
            buf0 = jnp.zeros((bp, CONV_B_W - 1, D_RNN), xp.dtype)
            h0 = jnp.zeros((bp, D_RNN), state_h.dtype)
            yp, nbp, hlp = rglru_mixer(xp, buf0, h0, b_w_in[j], b_conv_w[j], b_conv_b[j],
                                      b_gate_a_w[j], b_gate_a_b[j], b_gate_x_w[j], b_gate_x_b[j],
                                      b_lambda[j], b_w_out[j])
            ys, nbs, hls = rglru_mixer(xs, state_conv_b[j], state_h[j], b_w_in[j], b_conv_w[j], b_conv_b[j],
                                      b_gate_a_w[j], b_gate_a_b[j], b_gate_x_w[j], b_gate_x_b[j],
                                      b_lambda[j], b_w_out[j])
            conv_b_p.append(nbp)
            conv_b_s.append(nbs)
            h_p.append(hlp)
            h_s.append(hls)
        xp = layer_norm(ALPHA * xp + yp, ln1_g[i], ln1_b[i])
        xs = layer_norm(ALPHA * xs + ys, ln1_g[i], ln1_b[i])
        mp = hier_moe(xp, moe_w_group[i], moe_w_expert[i], moe_w_gate[i], moe_w_up[i], moe_w_down[i])
        ms = hier_moe(xs, moe_w_group[i], moe_w_expert[i], moe_w_gate[i], moe_w_up[i], moe_w_down[i])
        xp = layer_norm(ALPHA * xp + mp, ln2_g[i], ln2_b[i])
        xs = layer_norm(ALPHA * xs + ms, ln2_g[i], ln2_b[i])
    new_conv_a_prompt = jnp.stack(conv_a_p, axis=0)
    new_conv_a_sample = jnp.stack(conv_a_s, axis=0)
    new_conv_b_prompt = jnp.stack(conv_b_p, axis=0)
    new_conv_b_sample = jnp.stack(conv_b_s, axis=0)
    new_h_prompt = jnp.stack(h_p, axis=0)
    new_h_sample = jnp.stack(h_s, axis=0)
    return (xp, xs, new_conv_a_prompt, new_conv_a_sample, new_conv_b_prompt, new_conv_b_sample,
            new_h_prompt, new_h_sample)


_drawn_inputs = setup_inputs


def setup_inputs(seed=0):
    import zlib

    import numpy as np

    out = dict(_drawn_inputs(seed))
    spreads = {}
    factors = {'b_gate_a_b': 25.662, 'b_gate_x_b': 8.0}
    for name, (base, spread) in spreads.items():
        noise = np.random.default_rng([zlib.crc32(name.encode()), seed]).standard_normal(out[name].shape)
        drawn = base * np.exp(spread * noise) if base else spread * noise
        out[name] = __import__('jax').numpy.asarray(drawn.astype(out[name].dtype))
    for name, factor in factors.items():
        out[name] = (out[name] * factor).astype(out[name].dtype)
    return out
```

```python
from contextlib import ExitStack

import concourse.bass as bass
from concourse import mybir

F32 = mybir.dt.float32
BF16 = mybir.dt.bfloat16
I32 = mybir.dt.int32
ALU = mybir.AluOpType
ACT = mybir.ActivationFunctionType
AX = mybir.AxisListType.X

P = 128
D = 1024
KT = D // P
SEQ = 512
DEC = 8
T = SEQ + DEC
TT = 104
NT = T // TT
LAST = SEQ - (NT - 1) * TT
HALF = T // 2
DEPTH = 2
ALPHA = (2.0 * DEPTH) ** 0.25
LN_EPS = 1e-5
RG_C = 8.0
GELU_C = 0.7978845608028654
GELU_A = 0.044715
GROUPS = 4
EPG = 8
NE = GROUPS * EPG
TOPK = 2
FE = 512
FT = FE // P
ROWS = 64
OVER = T * TOPK // ROWS
NBLK = NE + OVER
MAXQ = -(-T // ROWS) - 1
RING = 9
SLOT = KT * FE
BIG = 1.0e30

WA, WB = 3, 4
R_SA = 0
R_WA = R_SA + DEC * (WA - 1)
R_SB = R_WA + WA
R_H = R_SB + DEC * (WB - 1)
R_WB = R_H + DEC
R_BB = R_WB + WB
R_GA = R_BB + 1
R_GX = R_GA + 1
R_LAM = R_GX + 1
NROW = R_LAM + 1

U_IN = (KT, KT // 2 + 1)
U_OUT = 2
POS_IN = (0, U_IN[0] + U_OUT + 3 * NE)
POS_OUT = (POS_IN[0] + U_IN[0], POS_IN[1] + U_IN[1])
POS_EXP = (POS_OUT[0] + U_OUT, POS_OUT[1] + U_OUT)
PEEL = 1
UNROLL = 3
TRIPS = (NE - 2 * PEEL) // UNROLL


def ring_slot(pos):
    return pos % RING


def unit_dmas(pos):
    if pos < U_IN[0]:
        return 3
    return 2 if POS_IN[1] <= pos < POS_OUT[1] else 1


def load_target(pos):
    return sum(16 * unit_dmas(p) for p in range(pos % RING, pos + 1, RING))


def residual_target(q, i):
    return 16 * (i // 2 + 1) + (16 if q == 0 and i == NT - 1 else 0)


def build(nc, a, outs):
    y_prompt, y_sample, na_p, na_s, nb_p, nb_s, nh_p, nh_s = outs
    with ExitStack() as ctx:
        def sb(name, shape, dt=F32):
            return ctx.enter_context(nc.sbuf_tensor(name, shape, dt))

        def sem(name):
            return ctx.enter_context(nc.semaphore(name))

        def sems(name, n):
            return [sem(f"{name}{i}") for i in range(n)]

        x1_dram = [nc.dram_tensor(f"x1_{l}", [T, D], F32).ap() for l in range(DEPTH)]
        x2_dram = nc.dram_tensor("x2_0", [T, D], F32).ap()
        rows_dram = nc.dram_tensor("yrows", [NBLK * ROWS, D], F32).ap()

        ring = sb("ring", [P, RING, SLOT])
        A = sb("A", [P, KT * T])
        Bt = sb("Bt", [P, KT * T])
        C = sb("C", [P, 6 * D])
        feat = sb("feat", [P, KT, NROW])
        wr = sb("wr", [P, KT, GROUPS + NE])
        ident = sb("ident", [P, P])
        conv0 = sb("conv0", [P, DEPTH, KT, DEC])
        spx = sb("spx", [P, 6, KT])
        new_cols = sb("new_cols", [P, KT, 20])
        before = sb("before", [TT, TT], BF16)
        ones = sb("ones", [TT, TT], BF16)
        iota = sb("iota", [TT, max(ROWS, NBLK)])
        thr = sb("thr", [TT, MAXQ])
        tokid = sb("tokid", [TT, NT])
        rev = sb("rev", [TT, NE])
        ones_f = sb("ones_f", [TT, NE])
        unused = sb("unused", [TT, DEPTH])
        half_neg = sb("half_neg", [TT, 1])
        wts = sb("wts", [TT, TOPK * NT])
        slot_i = sb("slot_i", [TT, TOPK * NT], I32)
        idx = sb("idx", [ROWS, NBLK], I32)
        cur = sb("cur", [ROWS, 1], I32)
        over_i = sb("over_i", [1, OVER + 1], I32)
        stat = sb("stat", [TT, 2, 16])

        ps = ctx.enter_context(nc.psum_tensor("ps", [P, 8, 512], F32))

        xT = A[:, :].rearrange("p (k t) -> p k t", k=KT)
        hT = Bt[:, :].rearrange("p (k t) -> p k t", k=KT)
        xtok = C[:TT, 0:NT * D].rearrange("p (i d) -> p i d", i=NT)
        rowt = Bt[:NROW, 0:D]
        tmp = [C[:, i * T:(i + 1) * T] for i in range(9)]
        pad = C[:, 9 * T:10 * T + WB - 1]
        zero = Bt[:, 3 * D:4 * D]
        gain, shift = C[:TT, 0:D], C[:TT, D:2 * D]
        zt = [C[:TT, (2 + i) * D:(3 + i) * D] for i in range(2)]
        res = [C[:TT, (4 + i) * D:(5 + i) * D] for i in range(2)]
        r1 = [Bt[:TT, i * D:(i + 1) * D] for i in range(2)]
        r2 = [Bt[:TT, (2 + i) * D:(3 + i) * D] for i in range(2)]
        x1T = [A[:, i * 832:(i + 1) * 832].rearrange("p (k t) -> p k t", k=KT) for i in range(2)]
        new_rows = A[:20, 2048:2048 + D]
        rt = [0]

        def route(shape):
            n = 1
            for s in shape[1:]:
                n *= s
            v = Bt[:shape[0], rt[0]:rt[0] + n]
            rt[0] += n
            if len(shape) == 3:
                v = v.rearrange("p (a b) -> p a b", a=shape[1])
            if len(shape) == 4:
                v = v.rearrange("p (a b c) -> p a b c", a=shape[1], b=shape[2])
            return v

        lg = route([TT, NT, GROUPS + NE])
        gsh = route([TT, NT, GROUPS])
        gex = route([TT, NT, GROUPS])
        ohg = route([TT, NT, GROUPS])
        elm = route([TT, NT, NE])
        key = route([TT, NT, NE])
        oh = route([TT, TOPK, NT, NE])
        s5 = route([TT, 16, NT])
        rank = route([TT, NT, NE])
        cnt = route([TT, NE])
        nbl = route([TT, NE])
        cum = route([TT, NE])
        start = route([TT, NE])
        s10 = route([TT, 12, TOPK * NT])
        cmpq = route([TT, TOPK * NT, MAXQ])
        rowhot = route([TT, TOPK * NT, ROWS])
        blkhot = route([TT, TOPK * NT, NBLK])
        big8 = route([TT, NE, MAXQ])
        prod = route([TT, TOPK, NT * NE])
        ovcmp = Bt[0:1, 0:OVER * NE].rearrange("p (a b) -> p a b", a=OVER)
        picked = sb("picked", [TT, NT, NE], BF16)
        assert rt[0] <= KT * T, rt[0]
        xg = [A[:ROWS, i * D:(i + 1) * D] for i in range(UNROLL)]
        xgT = A[:, 3 * D:3 * D + KT * ROWS].rearrange("p (k t) -> p k t", k=KT)
        gated = Bt[:, 0:FT * ROWS]
        h = Bt[:, 256:256 + FT * ROWS]
        yo = Bt[:ROWS, D:2 * D]

        x_in = sems("x_in", NT)
        row_in = sem("row_in")
        wr_in = sem("wr_in")
        zero_ok = sem("zero_ok")
        zero_out = sem("zero_out")
        pool_c = sem("pool_c")
        consts = sem("consts")
        dve_c = sem("dve_c")
        act_c = sem("act_c")
        setup_mm = sem("setup_mm")
        setup_dve = sem("setup_dve")
        setup_act = sem("setup_act")
        loaded = sems("loaded", RING)
        freed = sem("freed")
        L = range(DEPTH)
        mm_in = [sem(f"mm_in{l}") for l in L]
        mm_gate = sem("mm_gate")
        ev_a = [sem(f"ev_a{l}") for l in L]
        ev_b = [sem(f"ev_b{l}") for l in L]
        h_done = [sem(f"h_done{l}") for l in L]
        xc_done = sem("xc_done")
        lam_ok = sem("lam_ok")
        pad_ok = sem("pad_ok")
        sig_ok = sem("sig_ok")
        decay_ok = sem("decay_ok")
        gelu_in = sem("gelu_in")
        gelu_ok = sem("gelu_ok")
        sq_in = sem("sq_in")
        sq_ok = sem("sq_ok")
        st_mm = sem("st_mm")
        st_sb = sem("st_sb")
        out_mm = [sem(f"out_mm{l}") for l in L]
        par_in = [sem(f"par_in{l}") for l in range(2 * DEPTH)]
        res_in = [sem(f"res_in{l}_{j}") for l in range(2 * DEPTH) for j in range(2)]
        z_done = [sem(f"z_done{l}") for l in range(2 * DEPTH)]
        var_ok = [sem(f"var_ok{l}") for l in range(2 * DEPTH)]
        rstd_ok = [sem(f"rstd_ok{l}") for l in range(2 * DEPTH)]
        x_done = [sem(f"x_done{l}") for l in range(2 * DEPTH)]
        x_out = [[sem(f"x_out{q}_{j}") for j in range(2)] for q in range(2 * DEPTH)]
        turned = [sem(f"turned{l}") for l in range(3)]
        turned_sb = [sem(f"turned_sb{l}") for l in range(3)]
        logit_mm = sem("logit_mm")
        gsh_ok = sem("gsh_ok")
        gex_ok = sem("gex_ok")
        d_ok = sem("d_ok")
        e_ok = sem("e_ok")
        pick_ok = sem("pick_ok")
        rank_mm = sem("rank_mm")
        hot_ok = sem("hot_ok")
        idx_mm = sem("idx_mm")
        idx_ok = [sem(f"idx_ok{l}") for l in L]
        over_done = [sem(f"over_done{l}") for l in L]
        gath = [sem(f"gath{l}_{j}") for l in L for j in range(UNROLL)]
        t_mm = [sem(f"t_mm{l}") for l in L]
        t_sb = [sem(f"t_sb{l}") for l in L]
        gu_mm = [sem(f"gu_mm{l}") for l in L]
        silu_ok = [sem(f"silu_ok{l}") for l in L]
        hid_ok = [sem(f"hid_ok{l}") for l in L]
        y_mm = [sem(f"y_mm{l}") for l in L]
        y_act = [sem(f"y_act{l}") for l in L]
        y_dve = [sem(f"y_dve{l}") for l in L]
        y_out = [sem(f"y_out{l}") for l in L]
        v_cur = [sem(f"v_cur{l}") for l in L]
        v_load = [sem(f"v_load{l}") for l in L]
        v_gath = [sem(f"v_gath{l}") for l in L]
        v_tmm = [sem(f"v_tmm{l}") for l in L]
        v_tsb = [sem(f"v_tsb{l}") for l in L]
        v_gu = [sem(f"v_gu{l}") for l in L]
        v_silu = [sem(f"v_silu{l}") for l in L]
        v_hid = [sem(f"v_hid{l}") for l in L]
        v_y = [sem(f"v_y{l}") for l in L]
        v_ya = [sem(f"v_ya{l}") for l in L]
        v_yd = [sem(f"v_yd{l}") for l in L]
        v_out = [sem(f"v_out{l}") for l in L]
        pick_in = [sem(f"pick_in{l}_{j}") for l in L for j in range(2)]
        state_out = sem("state_out")

        w_in0 = a["a_w_in"][0].rearrange("(p k) (j m q) -> p k j m q", k=KT, j=3, m=KT)
        w_in1 = a["b_w_in"][0].rearrange("(p k) (j m q) -> p k j m q", k=KT, j=2, m=KT // 2)
        w_out = [w[0].rearrange("(k p) n -> p k n", p=P) for w in (a["a_w_out"], a["b_w_out"])]
        w_ga = a["b_gate_a_w"][0].rearrange("n p j -> p n j")
        w_gx = a["b_gate_x_w"][0].rearrange("n p j -> p n j")
        gates = [a["moe_w_gate"][l].rearrange("e (p k) f -> e p (k f)", k=KT) for l in L]
        ups = [a["moe_w_up"][l].rearrange("e (p k) f -> e p (k f)", k=KT) for l in L]
        downs = [a["moe_w_down"][l].rearrange("e (m p) n -> e p m n", p=P) for l in L]

        def prompt_rows(i):
            return TT if i < NT - 1 else LAST

        block = ctx.enter_context(nc.Block())

        @block.sync
        def _(sp):
            def room(pos, off=0):
                if pos >= RING:
                    sp.wait_ge(freed, pos - RING + 1 + off)

            def expert(l, pos, e, off=0):
                for u, w in enumerate((gates, ups, downs)):
                    room(pos + u, off)
                    s = ring_slot(pos + u)
                    out = ring[:, s, :] if u < 2 else ring[:, s, :].rearrange("p (m n) -> p m n", m=FT)
                    sp.dma_start(out, w[l][e]).then_inc(loaded[s], 16)

            def input_unit0(c):
                for j in range(3):
                    out = ring[:, ring_slot(c), :KT * 3 * P].rearrange("p (k j q) -> p k j q", k=KT, j=3)
                    sp.dma_start(out[:, :, j, :], w_in0[:, :, j, c, :]).then_inc(loaded[ring_slot(c)], 16)

            def input_unit1(m):
                pos = POS_IN[1] + m
                room(pos)
                for j in range(2):
                    out = ring[:, ring_slot(pos), :].rearrange("p (k j q) -> p k j q", k=KT, j=2)
                    sp.dma_start(out[:, :, j, :], w_in1[:, :, j, m, :]).then_inc(loaded[ring_slot(pos)], 16)

            for i in range(NT):
                n = prompt_rows(i)
                sp.dma_start(xtok[:n, i, :], a["x_prompt"][0, i * TT:i * TT + n, :]).then_inc(x_in[i], 16)
            sp.dma_start(xtok[LAST:TT, NT - 1, :], a["x_sample"][:, 0, :]).then_inc(x_in[NT - 1], 16)
            for l in L:
                if l == 0:
                    for c in range(KT):
                        input_unit0(c)
                else:
                    for m in range(KT // 2):
                        input_unit1(m)
                    pos = POS_IN[1] + KT // 2
                    room(pos)
                    for j, w in enumerate((w_ga, w_gx)):
                        out = ring[:, ring_slot(pos), j * D:(j + 1) * D].rearrange("p (n q) -> p n q", n=KT)
                        sp.dma_start(out, w).then_inc(loaded[ring_slot(pos)], 16)
                for u in range(U_OUT):
                    pos = POS_OUT[l] + u
                    room(pos)
                    out = ring[:, ring_slot(pos), :].rearrange("p (k n) -> p k n", k=KT)
                    sp.dma_start(out, w_out[l][:, :, u * 512:(u + 1) * 512]).then_inc(loaded[ring_slot(pos)], 16)
                expert(l, POS_EXP[l], 0)
                with sp.Fori(0, TRIPS) as i:
                    for j in range(UNROLL):
                        expert(l, POS_EXP[l] + 3 * (PEEL + j), i * UNROLL + (PEEL + j), i * (3 * UNROLL))
                expert(l, POS_EXP[l] + 3 * (NE - 1), NE - 1)
                sp.wait_ge(idx_ok[l], 2)
                n_over = sp.value_load(over_i[0:1, OVER:OVER + 1], min_val=0, max_val=OVER)
                with sp.If(n_over > 0):
                    sp.wait_ge(y_mm[l], NE)
                    with sp.Fori(0, n_over) as o:
                        sp.wait_ge(v_y[l], o + 1)
                        e = sp.value_load(over_i[0:1, bass.ds(o, 1)], min_val=0, max_val=NE - 1)
                        for u, w in enumerate((gates, ups, downs)):
                            out = ring[:, u, :] if u < 2 else ring[:, u, :].rearrange("p (m n) -> p m n", m=FT)
                            sp.dma_start(out, w[l][e]).then_inc(v_load[l], 16)
                    sp.wait_ge(over_done[l], 1)
                sp.nop()

        @block.gpsimd
        def _(pool):
            n = [0]

            def step(ins):
                n[0] += 1
                ins.then_inc(pool_c, 1)
                pool.wait_ge(pool_c, n[0])

            step(pool.memset(ident[:, :], 0.0))
            pool.memset(zero, 0.0).then_inc(zero_ok, 1)
            step(pool.memset(before[:, :], 1.0))
            pool.affine_select(out=ident[:, :], in_=ident[:, :], compare_op=ALU.not_equal, fill=1.0,
                               base=0, pattern=[[-1, P]], channel_multiplier=1).then_inc(consts, 1)
            pool.affine_select(out=before[:, :], in_=before[:, :], compare_op=ALU.is_gt, fill=0.0,
                               base=0, pattern=[[1, TT]], channel_multiplier=-1).then_inc(consts, 1)
            pool.memset(ones[:, :], 1.0).then_inc(consts, 1)
            pool.memset(half_neg[:, :], -0.5).then_inc(consts, 1)
            pool.memset(ones_f[:, :], 1.0).then_inc(consts, 1)
            pool.iota(iota[:, :], pattern=[[1, max(ROWS, NBLK)]], base=0, channel_multiplier=0,
                      allow_small_or_imprecise_dtypes=True).then_inc(consts, 1)
            pool.iota(thr[:, :], pattern=[[ROWS, MAXQ]], base=ROWS, channel_multiplier=0,
                      allow_small_or_imprecise_dtypes=True).then_inc(consts, 1)
            pool.iota(tokid[:, :], pattern=[[TT, NT]], base=0, channel_multiplier=1,
                      allow_small_or_imprecise_dtypes=True).then_inc(consts, 1)
            pool.iota(rev[:, :], pattern=[[-1, NE]], base=NE, channel_multiplier=0,
                      allow_small_or_imprecise_dtypes=True).then_inc(consts, 1)

            pool.wait_ge(consts, 9)

            def roots(q):
                for i in range(NT):
                    pool.wait_ge(var_ok[q], i + 1)
                    pool.tensor_tensor(stat[:, i % 2, 15:16], stat[:, i % 2, 14:15], half_neg[:, :],
                                       ALU.pow).then_inc(rstd_ok[q], 1)

            for l in L:
                roots(2 * l)
                for j in range(2):
                    pool.wait_ge(x_out[2 * l][j], 16 * ((NT + 1 - j) // 2))
                pool.wait_ge(logit_mm, NT * (l + 1))
                pool.wait_ge(idx_ok[l], 1)
                for e in range(NE):
                    if e >= UNROLL:
                        pool.wait_ge(t_mm[l], e - UNROLL + 1)
                    pool.indirect_dma_start(
                        out=xg[e % UNROLL], out_offset=None, in_=x1_dram[l],
                        in_offset=bass.IndirectOffsetOnAxis(ap=idx[:, e:e + 1], axis=0),
                    ).then_inc(gath[UNROLL * l + e % UNROLL], 16)
                pool.wait_ge(idx_ok[l], 2)
                n_over = pool.value_load(over_i[0:1, OVER:OVER + 1], min_val=0, max_val=OVER)
                with pool.If(n_over > 0):
                    pool.wait_ge(t_mm[l], NE)
                    with pool.Fori(0, n_over) as o:
                        pool.tensor_copy(cur[:, 0:1], idx[:, bass.ds(o + NE, 1)]).then_inc(v_cur[l], 1)
                        pool.wait_ge(v_cur[l], o * 2 + 1)
                        pool.tensor_tensor(unused[:, l:l + 1], half_neg[:, :], half_neg[:, :],
                                           ALU.mult).then_inc(v_cur[l], 1)
                        pool.indirect_dma_start(
                            out=xg[0], out_offset=None, in_=x1_dram[l],
                            in_offset=bass.IndirectOffsetOnAxis(ap=cur[:, 0:1], axis=0),
                        ).then_inc(v_gath[l], 16)
                        pool.wait_ge(v_y[l], o + 2)
                    pool.wait_ge(over_done[l], 1)
                pool.nop()
                pool.wait_ge(y_out[l], 16 * NE)
                q = 2 * l + 1
                for i in range(NT + 1):
                    if i < NT:
                        if i >= 2:
                            pool.wait_ge(z_done[q], i - 1)
                        for k, r in enumerate((r1, r2)):
                            c = k * NT + i
                            pool.indirect_dma_start(
                                out=r[i % 2], out_offset=None, in_=rows_dram,
                                in_offset=bass.IndirectOffsetOnAxis(ap=slot_i[:, c:c + 1], axis=0),
                            ).then_inc(pick_in[2 * l + i % 2], 16)
                    if i >= 1:
                        pool.wait_ge(var_ok[q], i)
                        p = (i - 1) % 2
                        pool.tensor_tensor(stat[:, p, 15:16], stat[:, p, 14:15], half_neg[:, :],
                                           ALU.pow).then_inc(rstd_ok[q], 1)

        @block.tensor
        def _(pe):
            def product(bank, lhs, rhs, first=False):
                for k in range(KT):
                    mm = pe.matmul(bank, lhs(k), rhs(k), start=(k == 0), stop=(k == KT - 1))
                    if k == 0 and first:
                        mm.then_inc(freed, 1)
                return mm

            def turn_tile(x, bank0, q, i):
                xv = x.rearrange("r (p k) -> r k p", k=KT)
                for k in range(KT):
                    mm = pe.transpose(ps[:, bank0 + k // 4, (k % 4) * TT:(k % 4 + 1) * TT], xv[:, k, :],
                                      ident[:TT, :TT])
                return mm

            pe.wait_ge(consts, 1)
            for i in range(NT):
                pe.wait_ge(x_in[i], 16 if i < NT - 1 else 32)
                if i >= 4:
                    pe.wait_ge(setup_dve, i - 3)
                    pe.wait_ge(setup_act, i - 3)
                turn_tile(xtok[:, i, :], 2 * (i % 4), 0, i).then_inc(setup_mm, 1)
            pe.wait_ge(row_in, 16 * 9)
            pe.wait_ge(setup_dve, 2)
            for c in range(KT):
                mm = pe.transpose(ps[:, 2, c * NROW:(c + 1) * NROW], rowt[:, c * P:(c + 1) * P],
                                  ident[:NROW, :NROW])
            mm.then_inc(setup_mm, 1)
            pe.wait_ge(setup_dve, NT + 1)
            pe.wait_ge(setup_act, NT)

            for c in range(KT):
                s = ring_slot(c)
                pe.wait_ge(loaded[s], load_target(c))
                for jj, j in enumerate((1, 2, 0)):
                    n = 3 * c + jj
                    if n >= 4:
                        pe.wait_ge((ev_a[0], ev_b[0], h_done[0])[(n - 4) % 3], (n - 4) // 3 + 1)
                    for hf in range(2):
                        mm = product(ps[:, 2 * (n % 4) + hf, :HALF],
                                     lambda k: ring[:, s, (k * 3 + j) * P:(k * 3 + j + 1) * P],
                                     lambda k: xT[:, k, hf * HALF:(hf + 1) * HALF],
                                     first=(c > 0 and jj == 0 and hf == 0))
                    mm.then_inc(mm_in[0], 1)

            for l in L:
                if l == 1:
                    def rg_gates(c):
                        s = ring_slot(POS_IN[1] + KT // 2)
                        pe.wait_ge(xc_done, c + 1)
                        if c == 0:
                            pe.wait_ge(loaded[s], load_target(POS_IN[1] + KT // 2))
                        else:
                            pe.wait_ge(sig_ok, 2 * c)
                        for g in range(2):
                            for hf in range(2):
                                mm = pe.matmul(ps[:, 4 + 2 * g + hf, :HALF],
                                               ring[:, s, g * D + c * P:g * D + (c + 1) * P],
                                               tmp[6 + c % 2][:, hf * HALF:(hf + 1) * HALF],
                                               start=True, stop=True)
                                if c == KT - 1 and g == 0 and hf == 0:
                                    mm.then_inc(freed, 1)
                            mm.then_inc(mm_gate, 1)

                    pe.wait_ge(turned_sb[1], NT)
                    for c in range(KT):
                        pos = POS_IN[1] + c // 2
                        s = ring_slot(pos)
                        pe.wait_ge(loaded[s], load_target(pos))
                        for jj, j in enumerate((1, 0)):
                            if c >= 1:
                                pe.wait_ge((ev_a[1], ev_b[1])[jj], c)
                            for hf in range(2):
                                col = j * 2 * P + (c % 2) * P
                                mm = product(ps[:, 2 * jj + hf, :HALF],
                                             lambda k: ring[:, s, k * FE + col:k * FE + col + P],
                                             lambda k: xT[:, k, hf * HALF:(hf + 1) * HALF],
                                             first=(c % 2 == 0 and jj == 0 and hf == 0))
                            mm.then_inc(mm_in[1], 1)
                        if c >= 1:
                            rg_gates(c - 1)
                    rg_gates(KT - 1)

                q = 2 * l
                n_new = (10, 20)[l]

                def turn(i):
                    pe.wait_ge(x_done[q], i + 1)
                    if i >= 1:
                        pe.wait_ge(turned_sb[q], i)
                    turn_tile(zt[i % 2], 4, q, i).then_inc(turned[q], 1)

                def logits(i):
                    pe.wait_ge(turned_sb[q], i + 1)
                    for k in range(KT):
                        mm = pe.matmul(ps[:TT, 6, i * (GROUPS + NE):(i + 1) * (GROUPS + NE)],
                                       x1T[i % 2][:, k, :], wr[:, k, :], start=(k == 0), stop=(k == KT - 1))
                    mm.then_inc(logit_mm, 1)

                pe.wait_ge(h_done[l], KT)
                for i in range(NT):
                    if i >= 2:
                        pe.wait_ge(z_done[q], i - 1)
                    for nh in range(2):
                        s = ring_slot(POS_OUT[l] + nh)
                        if i == 0:
                            pe.wait_ge(loaded[s], load_target(POS_OUT[l] + nh))
                        mm = product(ps[:TT, 2 * (i % 2) + nh, :],
                                     lambda k: hT[:, k, i * TT:(i + 1) * TT],
                                     lambda k: ring[:, s, k * 512:(k + 1) * 512],
                                     first=(i == 0 and nh == 0))
                        if i == NT - 1 and nh == 0:
                            mm.then_inc(freed, 1)
                    mm.then_inc(out_mm[l], 1)
                    if i == 0:
                        for c in range(KT):
                            mm = pe.transpose(ps[:n_new, 6 + c // 4, (c % 4) * P:(c % 4 + 1) * P],
                                              new_cols[:, c, :n_new], ident[:, :])
                        mm.then_inc(st_mm, 1)
                    if i >= 1:
                        turn(i - 1)
                    if i == 2:
                        pe.wait_ge(st_sb, l + 1)
                        pe.wait_ge(wr_in, 32 * (l + 1))
                    if i >= 2:
                        logits(i - 2)
                logits(NT - 2)
                turn(NT - 1)
                logits(NT - 1)

                pe.wait_ge(pick_ok, l + 1)
                pe.wait_ge(consts, 9)
                for i in range(NT):
                    for j in range(i + 1):
                        pe.matmul(ps[:TT, 7, i * NE:(i + 1) * NE], (ones if j < i else before)[:, :],
                                  picked[:, j, :], start=(j == 0), stop=(j == i))
                for j in range(NT):
                    mm = pe.matmul(ps[:TT, 7, NT * NE:(NT + 1) * NE], ones[:, :], picked[:, j, :],
                                   start=(j == 0), stop=(j == NT - 1))
                mm.then_inc(rank_mm, 1)
                pe.wait_ge(hot_ok, l + 1)
                for c in range(TOPK * NT):
                    mm = pe.matmul(ps[:ROWS, 5, :NBLK], rowhot[:, c, :], blkhot[:, c, :],
                                   start=(c == 0), stop=(c == TOPK * NT - 1))
                mm.then_inc(idx_mm, 1)

                def turn_rows(x, done):
                    xv = x.rearrange("r (p k) -> r k p", k=KT)
                    for k in range(KT):
                        mm = pe.transpose(ps[:, 0, k * ROWS:(k + 1) * ROWS], xv[:, k, :], ident[:ROWS, :ROWS])
                    mm.then_inc(done, 1)

                def gate_up(slots, done, free):
                    for u in range(2):
                        for m in range(FT):
                            for k in range(KT):
                                mm = pe.matmul(ps[:, 1, (u * FT + m) * ROWS:(u * FT + m + 1) * ROWS],
                                               ring[:, slots[u], k * FE + m * P:k * FE + (m + 1) * P],
                                               xgT[:, k, :], start=(k == 0), stop=(k == KT - 1))
                                if free and u == 0 and (m, k) in ((0, 0), (FT - 1, KT - 1)):
                                    mm.then_inc(freed, 1)
                    mm.then_inc(done, 1)

                def down(slot, done, free):
                    for nh in range(2):
                        for m in range(FT):
                            mm = pe.matmul(ps[:ROWS, 2 + nh, :], h[:, m * ROWS:(m + 1) * ROWS],
                                           ring[:, slot, m * D + nh * 512:m * D + (nh + 1) * 512],
                                           start=(m == 0), stop=(m == FT - 1))
                            if free and nh == 0 and m == 0:
                                mm.then_inc(freed, 1)
                    mm.then_inc(done, 1)

                def expert(e, e0, trip=0, more=True):
                    pos = POS_EXP[l] + 3 * e0
                    slots = [ring_slot(pos + u) for u in range(3)]
                    pe.wait_ge(t_sb[l], e + 1)
                    for u in range(2):
                        pe.wait_ge(loaded[slots[u]], load_target(pos + u) + trip * 16)
                    b = (e0 + 1) % UNROLL
                    if more:
                        pe.wait_ge(gath[UNROLL * l + b], 16 * ((e0 + 1) // UNROLL + 1) + trip * 16)
                    gate_up(slots, gu_mm[l], True)
                    if more:
                        turn_rows(xg[b], t_mm[l])
                    pe.wait_ge(loaded[slots[2]], load_target(pos + 2) + trip * 16)
                    pe.wait_ge(hid_ok[l], e + 1)
                    pe.wait_ge(y_act[l], e)
                    pe.wait_ge(y_dve[l], e)
                    down(slots[2], y_mm[l], True)

                pe.wait_ge(gath[UNROLL * l], 16)
                turn_rows(xg[0], t_mm[l])
                expert(0, 0)
                with pe.Fori(0, TRIPS) as i:
                    for j in range(UNROLL):
                        expert(i * UNROLL + (PEEL + j), PEEL + j, i)
                expert(NE - 1, NE - 1, more=False)
                pe.wait_ge(idx_ok[l], 2)
                n_over = pe.value_load(over_i[0:1, OVER:OVER + 1], min_val=0, max_val=OVER)
                with pe.If(n_over > 0):
                    pe.wait_ge(y_act[l], NE)
                    pe.wait_ge(y_dve[l], NE)
                    pe.matmul(ps[:ROWS, 1, :ROWS], ident[:, :ROWS], ident[:, :ROWS], start=True,
                              stop=True).then_inc(v_y[l], 1)
                    with pe.Fori(0, n_over) as o:
                        pe.wait_ge(v_gath[l], o * 16 + 16)
                        pe.matmul(ps[:ROWS, 1, :ROWS], ident[:, :ROWS], ident[:, :ROWS], start=True, stop=True)
                        turn_rows(xg[0], v_tmm[l])
                        pe.wait_ge(v_tsb[l], o + 1)
                        pe.wait_ge(v_load[l], o * 48 + 48)
                        gate_up((0, 1), v_gu[l], False)
                        pe.wait_ge(v_hid[l], o + 1)
                        down(2, v_y[l], False)
                        pe.wait_ge(v_ya[l], o + 1)
                        pe.wait_ge(v_yd[l], o + 1)
                pe.nop()
                if l == 0:
                    for i in range(NT):
                        pe.wait_ge(x_done[1], i + 1)
                        if i >= 1:
                            pe.wait_ge(turned_sb[1], i)
                        turn_tile(zt[i % 2], 4, 1, i).then_inc(turned[1], 1)

        @block.scalar
        def _(act):
            n = [0]

            def step(ins):
                n[0] += 1
                ins.then_inc(act_c, 1)
                act.wait_ge(act_c, n[0])

            def rows_in(r, k, src):
                act.dma_start(rowt[r:r + k, :], src).then_inc(row_in, 16)

            rows_in(R_SA, DEC * 2, a["state_conv_a"][0].rearrange("b w d -> (b w) d"))
            rows_in(R_WA, WA, a["a_conv_w"][0])
            rows_in(R_SB, DEC * 3, a["state_conv_b"][0].rearrange("b w d -> (b w) d"))
            rows_in(R_H, DEC, a["state_h"][0])
            rows_in(R_WB, WB, a["b_conv_w"][0])
            for r, name in ((R_BB, "b_conv_b"), (R_GA, "b_gate_a_b"), (R_GX, "b_gate_x_b"), (R_LAM, "b_lambda")):
                rows_in(r, 1, a[name])

            def router_weights(l):
                for name, lo, hi in (("moe_w_group", 0, GROUPS), ("moe_w_expert", GROUPS, GROUPS + NE)):
                    act.dma_start(wr[:, :, lo:hi],
                                  a[name][l].rearrange("(p k) g -> p k g", k=KT)).then_inc(wr_in, 16)

            router_weights(0)
            act.dma_start(na_s[0, :, 0, :], a["state_conv_a"][0, :, 1, :]).then_inc(state_out, 16)
            act.dma_start(nb_s[0, :, 0:2, :], a["state_conv_b"][0, :, 1:3, :]).then_inc(state_out, 16)

            act.wait_ge(zero_ok, 1)
            for i in range(NE * ROWS, NBLK * ROWS, P):
                act.dma_start(rows_dram[i:i + P, :], zero).then_inc(zero_out, 16)

            for i in range(NT):
                act.wait_ge(setup_mm, i + 1)
                act.activation(xT[:, 4:8, i * TT:(i + 1) * TT],
                               ps[:, 2 * (i % 4) + 1, :4 * TT].rearrange("p (k t) -> p k t", k=4),
                               ACT.Copy).then_inc(setup_act, 1)
            act.wait_ge(lam_ok, 1)
            act.activation(spx[:, 2, :], spx[:, 1, :], ACT.Exp, scale=-1.0).then_inc(lam_ok, 1)

            def halves(v):
                return v.rearrange("p (a b) -> p a b", a=2)

            def banks(pair):
                return ps[:, 2 * pair:2 * pair + 2, :HALF]

            for c in range(KT):
                act.wait_ge(mm_in[0], 3 * c + 1)
                if c >= 2:
                    act.wait_ge(ev_b[0], c - 1)
                act.activation(halves(tmp[c % 2]), banks((3 * c) % 4), ACT.Copy).then_inc(ev_a[0], 1)

            for l in L:
                if l == 1:
                    def recurrence_gates(c):
                        act.wait_ge(mm_gate, 2 * c + 1)
                        if c >= 1:
                            act.wait_ge(h_done[1], c)
                        act.activation(halves(tmp[2]), banks(2), ACT.Sigmoid,
                                       bias=feat[:, c, R_GA:R_GA + 1]).then_inc(sig_ok, 1)
                        act.wait_ge(mm_gate, 2 * c + 2)
                        act.activation(halves(tmp[3]), banks(3), ACT.Sigmoid,
                                       bias=feat[:, c, R_GX:R_GX + 1]).then_inc(sig_ok, 1)
                        act.wait_ge(sig_ok, 2 * c + 2)
                        act.activation(tmp[4], tmp[2], ACT.Exp, scale=spx[:, 0, c:c + 1]).then_inc(decay_ok, 1)
                        act.activation(tmp[5], tmp[2], ACT.Tanh, scale=spx[:, 0, c:c + 1]).then_inc(decay_ok, 1)
                        act.wait_ge(gelu_in, c + 1)
                        act.activation(tmp[8], tmp[8], ACT.Tanh, scale=GELU_C).then_inc(gelu_ok, 1)
                        act.wait_ge(sq_in, c + 1)
                        act.activation(tmp[2], tmp[2], ACT.Sqrt).then_inc(sq_ok, 1)

                    act.wait_ge(lam_ok, 3)
                    for c in range(KT):
                        act.wait_ge(mm_in[1], 2 * c + 1)
                        act.wait_ge(xc_done, c) if c >= 1 else act.wait_ge(pad_ok, 2)
                        act.activation(pad[:, WB - 1:].rearrange("p (a b) -> p a b", a=2), banks(0),
                                       ACT.Copy).then_inc(ev_a[1], 1)
                        act.wait_ge(mm_in[1], 2 * c + 2)
                        if c >= 2:
                            act.wait_ge(h_done[1], c - 1)
                        act.activation(halves(tmp[c % 2]), banks(1), ACT.Copy).then_inc(ev_b[1], 1)
                        if c >= 1:
                            recurrence_gates(c - 1)
                    recurrence_gates(KT - 1)

                def norm_loads(q):
                    g, b = (a["ln1_g"], a["ln1_b"]) if q % 2 == 0 else (a["ln2_g"], a["ln2_b"])
                    act.dma_start(gain, g[q // 2:q // 2 + 1, :].broadcast_to([TT, D])).then_inc(par_in[q], 16)
                    act.dma_start(shift, b[q // 2:q // 2 + 1, :].broadcast_to([TT, D])).then_inc(par_in[q], 16)

                def residual(q, i):
                    if i >= 2:
                        act.wait_ge(z_done[q], i - 1)
                    n = prompt_rows(i)
                    if q == 0:
                        act.dma_start(res[i % 2][:n], a["x_prompt"][0, i * TT:i * TT + n, :]).then_inc(res_in[2 * q + i % 2], 16)
                        if n < TT:
                            act.dma_start(res[i % 2][n:], a["x_sample"][:, 0, :]).then_inc(res_in[2 * q + i % 2], 16)
                    else:
                        src = (None, x1_dram[0], x2_dram, x1_dram[1])[q]
                        act.dma_start(res[i % 2], src[i * TT:(i + 1) * TT, :]).then_inc(res_in[2 * q + i % 2], 16)

                q = 2 * l
                act.wait_ge(h_done[l], KT)
                if l == 1:
                    for j in range(2):
                        act.wait_ge(x_out[1][j], 16 * ((NT + 1 - j) // 2))
                norm_loads(q)
                residual(q, 0)
                residual(q, 1)

                act.wait_ge(st_mm, l + 1)
                n_new = (10, 20)[l]
                act.activation(new_rows[:n_new].rearrange("r (a b) -> r a b", a=2), ps[:n_new, 6:8, :],
                               ACT.Copy).then_inc(st_sb, 1)
                act.wait_ge(st_sb, l + 1)
                if l == 0:
                    act.dma_start(na_p[0, 0], new_rows[0:2]).then_inc(state_out, 16)
                    act.dma_start(na_s[0, :, 1, :], new_rows[2:10]).then_inc(state_out, 16)
                else:
                    act.dma_start(nb_p[0, 0], new_rows[0:3]).then_inc(state_out, 16)
                    act.dma_start(nb_s[0, :, 2, :], new_rows[3:11]).then_inc(state_out, 16)
                    act.dma_start(nh_p[0], new_rows[11:12]).then_inc(state_out, 16)
                    act.dma_start(nh_s[0], new_rows[12:20]).then_inc(state_out, 16)

                for i in range(NT):
                    act.wait_ge(x_done[q], i + 1)
                    act.dma_start(x1_dram[l][i * TT:(i + 1) * TT, :], zt[i % 2]).then_inc(x_out[q][i % 2], 16)
                    act.wait_ge(turned[q], i + 1)
                    if i >= 2:
                        act.wait_ge(logit_mm, NT * l + i - 1)
                    act.activation(x1T[i % 2].rearrange("p (a k) t -> p a (k t)", a=2), ps[:, 4:6, :4 * TT],
                                   ACT.Copy).then_inc(turned_sb[q], 1)
                    if i + 2 < NT:
                        residual(q, i + 2)

                act.wait_ge(gsh_ok, l + 1)
                act.activation(gex, gsh, ACT.Exp).then_inc(gex_ok, 1)
                act.wait_ge(d_ok, l + 1)
                act.activation(s5[:, 8, :], s5[:, 7, :], ACT.Exp).then_inc(e_ok, 1)

                q = 2 * l + 1
                for j in range(2):
                    act.wait_ge(x_out[2 * l][j], 16 * ((NT + 1 - j) // 2))
                norm_loads(q)
                residual(q, 0)
                residual(q, 1)
                if l == 0:
                    act.wait_ge(logit_mm, NT)
                    router_weights(1)

                act.wait_ge(idx_ok[l], 2)

                def expert(e):
                    act.wait_ge(gu_mm[l], e + 1)
                    act.wait_ge(hid_ok[l], e)
                    act.activation(gated, ps[:, 1, :FT * ROWS], ACT.Silu).then_inc(silu_ok[l], 1)
                    act.wait_ge(y_mm[l], e + 1)
                    act.wait_ge(y_out[l], e * 16)
                    act.activation(yo[:, :512], ps[:ROWS, 2, :], ACT.Copy).then_inc(y_act[l], 1)
                    act.wait_ge(y_act[l], e + 1)
                    act.wait_ge(y_dve[l], e + 1)
                    act.dma_start(rows_dram[bass.ds(e * ROWS, ROWS), :], yo).then_inc(y_out[l], 16)

                expert(0)
                with act.Fori(0, TRIPS) as i:
                    for j in range(UNROLL):
                        expert(i * UNROLL + (PEEL + j))
                expert(NE - 1)
                n_over = act.value_load(over_i[0:1, OVER:OVER + 1], min_val=0, max_val=OVER)
                with act.If(n_over > 0):
                    act.wait_ge(y_out[l], 16 * NE)
                    with act.Fori(0, n_over) as o:
                        act.wait_ge(v_gu[l], o + 1)
                        act.activation(gated, ps[:, 1, :FT * ROWS], ACT.Silu).then_inc(v_silu[l], 1)
                        act.wait_ge(v_y[l], o + 2)
                        act.activation(yo[:, :512], ps[:ROWS, 2, :], ACT.Copy).then_inc(v_ya[l], 1)
                        act.wait_ge(v_ya[l], o + 1)
                        act.wait_ge(v_yd[l], o + 1)
                        act.dma_start(rows_dram[bass.ds(o * ROWS + NE * ROWS, ROWS), :], yo).then_inc(v_out[l], 16)
                        act.wait_ge(v_out[l], o * 16 + 16)
                act.nop()

                for i in range(NT):
                    act.wait_ge(x_done[q], i + 1)
                    rows = prompt_rows(i)
                    if l == 0:
                        act.dma_start(x2_dram[i * TT:(i + 1) * TT, :], zt[i % 2]).then_inc(x_out[q][i % 2], 16)
                        act.wait_ge(turned[1], i + 1)
                        act.activation(xT[:, :, i * TT:(i + 1) * TT],
                                       ps[:, 4:6, :4 * TT].rearrange("p a (k t) -> p a k t", k=4),
                                       ACT.Copy).then_inc(turned_sb[1], 1)
                    else:
                        act.dma_start(y_prompt[0, i * TT:i * TT + rows, :], zt[i % 2][:rows]).then_inc(x_out[q][i % 2], 16)
                        if rows < TT:
                            act.dma_start(y_sample[:, 0, :], zt[i % 2][rows:]).then_inc(x_out[q][i % 2], 16)
                    if i + 2 < NT:
                        residual(q, i + 2)
            act.wait_ge(x_out[3][0], 16 * 4)
            act.wait_ge(x_out[3][1], 16 * 2)
            act.wait_ge(state_out, 16 * 8)

        @block.vector
        def _(dve):
            n = [0]

            def step(ins):
                n[0] += 1
                ins.then_inc(dve_c, 1)
                dve.wait_ge(dve_c, n[0])

            def tsc(out, x, s1, op, s2=None, op1=None):
                return dve.tensor_scalar(out, x, s1, s2, op, op1) if op1 else dve.tensor_scalar(out, x, s1, None, op)

            tt, stt = dve.tensor_tensor, dve.scalar_tensor_tensor

            for i in range(NT):
                dve.wait_ge(setup_mm, i + 1)
                dve.tensor_copy(xT[:, 0:4, i * TT:(i + 1) * TT],
                                ps[:, 2 * (i % 4), :4 * TT].rearrange("p (k t) -> p k t", k=4)).then_inc(setup_dve, 1)
            dve.wait_ge(setup_mm, NT + 1)
            dve.tensor_copy(feat[:, :, :], ps[:, 2, :KT * NROW].rearrange("p (c r) -> p c r", c=KT)
                            ).then_inc(setup_dve, 1)
            dve.wait_ge(setup_dve, NT + 1)

            lam = feat[:, :, R_LAM]
            step(tsc(spx[:, 3, :], lam, -1.0, ALU.mult))
            tt(spx[:, 1, :], spx[:, 3, :], lam, ALU.max).then_inc(lam_ok, 1)
            dve.wait_ge(lam_ok, 2)
            u, s, s2, y = spx[:, 2, :], spx[:, 4, :], spx[:, 5, :], spx[:, 0, :]
            step(tsc(s2, u, 2.0, ALU.add))
            step(dve.reciprocal(s, s2))
            step(tt(s, s, u, ALU.mult))
            step(tt(s2, s, s, ALU.mult))
            step(tsc(y, s2, 1.0 / 17, ALU.mult))
            for k in range(7, 0, -1):
                step(stt(y, y, 1.0 / (2 * k + 1), s2, ALU.add, ALU.mult))
            step(stt(y, y, 1.0, s, ALU.add, ALU.mult))
            step(tsc(s, spx[:, 3, :], 0.0, ALU.max))
            step(stt(y, y, 2.0, s, ALU.mult, ALU.add))
            tsc(y, y, -RG_C, ALU.mult).then_inc(lam_ok, 1)

            def state_taps(l, r_state, r_w, taps):
                out = conv0[:, l, :, :]
                for w in range(taps):
                    st = feat[:, :, r_state + w:r_state + DEC * taps:taps]
                    wv = feat[:, :, r_w + w:r_w + w + 1].broadcast_to([P, KT, DEC])
                    t = out if w == 0 else tmp[4][:, :KT * DEC].rearrange("p (c s) -> p c s", c=KT)
                    step(tt(t, st, wv, ALU.mult))
                    if w:
                        step(tt(out, out, t, ALU.add))
                if l == 1:
                    bv = feat[:, :, R_BB:R_BB + 1].broadcast_to([P, KT, DEC])
                    step(tt(out, out, bv, ALU.add))

            state_taps(0, R_SA, R_WA, WA - 1)
            state_taps(1, R_SB, R_WB, WB - 1)
            dve.memset(pad[:, :WA - 1], 0.0).then_inc(pad_ok, 1)
            dve.wait_ge(pad_ok, 1)

            def halves(v):
                return v.rearrange("p (a b) -> p a b", a=2)

            def banks(pair):
                return ps[:, 2 * pair:2 * pair + 2, :HALF]

            def tap(r, c):
                return feat[:, c, r:r + 1]

            for c in range(KT):
                dve.wait_ge(mm_in[0], 3 * c + 2)
                dve.wait_ge(ev_a[0], c + 1)
                u = pad[:, WA - 1:WA - 1 + T]
                tt(halves(u), banks((3 * c + 1) % 4), halves(tmp[c % 2]), ALU.mult).then_inc(ev_b[0], 1)
                dve.wait_ge(ev_b[0], c + 1)
                dve.tensor_copy(new_cols[:, c, :10], pad[:, SEQ:SEQ + 10])
                step(tsc(tmp[2][:, :SEQ], pad[:, :SEQ], tap(R_WA, c), ALU.mult))
                dve.tensor_copy(tmp[2][:, SEQ:], conv0[:, 0, c, :])
                step(stt(tmp[2][:, :SEQ], pad[:, 1:SEQ + 1], tap(R_WA + 1, c), tmp[2][:, :SEQ], ALU.mult, ALU.add))
                step(stt(tmp[3], u, tap(R_WA + 2, c), tmp[2], ALU.mult, ALU.add))
                dve.wait_ge(mm_in[0], 3 * c + 3)
                if c * T + T > 3 * D:
                    dve.wait_ge(zero_out, 16 * (OVER * ROWS // P))
                tt(halves(hT[:, c, :]), banks((3 * c + 2) % 4), halves(tmp[3]), ALU.mult).then_inc(h_done[0], 1)

            def norm(q, i):
                z, st = zt[i % 2], stat[:, i % 2, :]
                dve.wait_ge(z_done[q], i + 1)
                dve.bn_stats(st[:, 0:6], z[:, :512])
                step(dve.bn_stats(st[:, 6:12], z[:, 512:]))
                step(dve.bn_aggr(st[:, 12:14], st[:, 0:12]))
                tsc(st[:, 14:15], st[:, 13:14], LN_EPS, ALU.add).then_inc(var_ok[q], 1)
                dve.wait_ge(rstd_ok[q], i + 1)
                step(tsc(z, z, st[:, 12:13], ALU.subtract, st[:, 15:16], ALU.mult))
                if i == 0:
                    dve.wait_ge(par_in[q], 32)
                step(tt(z, z, gain, ALU.mult))
                tt(z, z, shift, ALU.add).then_inc(x_done[q], 1)

            def free_tile(q, i, is_turned):
                if i >= 2:
                    dve.wait_ge(x_out[q][i % 2], 16 * (i // 2))
                    if is_turned:
                        dve.wait_ge(turned[q], i - 1)

            for l in L:
                if l == 1:
                    R, I, DEC_A, TH, G1 = tmp[2], tmp[3], tmp[4], tmp[5], tmp[8]
                    dve.wait_ge(turned[1], NT)
                    for j in range(2):
                        dve.wait_ge(x_out[1][j], 16 * ((NT + 1 - j) // 2))
                    dve.memset(pad[:, :WB - 1], 0.0).then_inc(pad_ok, 1)

                    def conv(c):
                        x = tmp[6 + c % 2]
                        dve.wait_ge(ev_a[1], c + 1)
                        if c >= 2:
                            dve.wait_ge(h_done[1], c - 1)
                        dve.tensor_copy(new_cols[:, c, :11], pad[:, SEQ:SEQ + 11])
                        step(tsc(G1[:, :SEQ], pad[:, :SEQ], tap(R_WB, c), ALU.mult, tap(R_BB, c), ALU.add))
                        step(stt(G1[:, :SEQ], pad[:, 1:SEQ + 1], tap(R_WB + 1, c), G1[:, :SEQ], ALU.mult, ALU.add))
                        dve.tensor_copy(G1[:, SEQ:], conv0[:, 1, c, :])
                        step(stt(G1[:, :SEQ], pad[:, 2:SEQ + 2], tap(R_WB + 2, c), G1[:, :SEQ], ALU.mult, ALU.add))
                        stt(x, pad[:, WB - 1:], tap(R_WB + 3, c), G1, ALU.mult, ALU.add).then_inc(xc_done, 1)
                        dve.wait_ge(xc_done, c + 1)

                    def recurrence(c):
                        x, g = tmp[6 + c % 2], tmp[c % 2]
                        if c >= 1:
                            dve.wait_ge(h_done[1], c)
                        dve.wait_ge(ev_b[1], c + 1)
                        step(tt(G1, g, g, ALU.mult))
                        step(tsc(G1, G1, GELU_A, ALU.mult, 1.0, ALU.add))
                        tt(G1, G1, g, ALU.mult).then_inc(gelu_in, 1)
                        dve.wait_ge(sig_ok, 2 * c + 2)
                        step(tt(I, I, x, ALU.mult))
                        dve.wait_ge(decay_ok, 2 * c + 2)
                        step(stt(R, DEC_A, -1.0, DEC_A, ALU.mult, ALU.mult))
                        stt(R, R, -1.0, TH, ALU.add, ALU.mult).then_inc(sq_in, 1)
                        dve.wait_ge(gelu_ok, c + 1)
                        step(stt(G1, G1, 1.0, g, ALU.add, ALU.mult))
                        dve.wait_ge(sq_ok, c + 1)
                        step(tt(I, I, R, ALU.mult))
                        step(tt(TH[:, SEQ:], DEC_A[:, SEQ:], feat[:, c, R_H:R_H + DEC], ALU.mult))
                        step(tt(TH[:, SEQ:], TH[:, SEQ:], I[:, SEQ:], ALU.add))
                        step(dve.tensor_tensor_scan(TH[:, :SEQ], DEC_A[:, :SEQ], I[:, :SEQ], 0.0, ALU.mult, ALU.add))
                        dve.tensor_copy(new_cols[:, c, 11:20], TH[:, SEQ - 1:])
                        stt(hT[:, c, :], G1, 0.5, TH, ALU.mult, ALU.mult).then_inc(h_done[1], 1)

                    for c in range(KT):
                        conv(c)
                        if c >= 1:
                            recurrence(c - 1)
                    recurrence(KT - 1)

                q = 2 * l
                for i in range(NT):
                    free_tile(q, i, True)
                    dve.wait_ge(res_in[2 * q + i % 2], residual_target(q, i))
                    dve.wait_ge(out_mm[l], i + 1)
                    stt(zt[i % 2].rearrange("r (a b) -> r a b", a=2), res[i % 2].rearrange("r (a b) -> r a b", a=2),
                        ALPHA, ps[:TT, 2 * (i % 2):2 * (i % 2) + 2, :], ALU.mult, ALU.add).then_inc(z_done[q], 1)
                    norm(q, i)

                dve.wait_ge(logit_mm, NT * (l + 1))
                dve.wait_ge(consts, 9)
                step(dve.tensor_copy(lg, ps[:TT, 6, :NT * (GROUPS + NE)].rearrange("p (i c) -> p i c", i=NT)))
                gl, el = lg[:, :, :GROUPS], lg[:, :, GROUPS:]

                def v5(k):
                    return s5[:, k, :]

                def over(v, n_):
                    return v.unsqueeze(2).broadcast_to([TT, NT, n_])

                def ranks(n_):
                    return rev[:, NE - n_:].unsqueeze(1).broadcast_to([TT, NT, n_])

                step(dve.tensor_reduce(v5(0), gl, AX, ALU.max))
                tt(gsh, gl, over(v5(0), GROUPS), ALU.subtract).then_inc(gsh_ok, 1)
                dve.wait_ge(gsh_ok, l + 1)
                step(tsc(ohg, gsh, 0.0, ALU.is_equal))
                step(tt(ohg, ohg, ranks(GROUPS), ALU.mult))
                step(dve.tensor_reduce(v5(1), ohg, AX, ALU.max))
                step(tt(ohg, over(v5(1), GROUPS), ranks(GROUPS), ALU.is_equal))
                dve.wait_ge(gex_ok, l + 1)
                step(dve.tensor_reduce(v5(2), gex, AX, ALU.add))
                step(dve.reciprocal(v5(3), v5(2)))
                step(tsc(ohg, ohg, BIG, ALU.mult, -BIG, ALU.add))
                for i in range(NT):
                    ins = tt(elm[:, i, :].rearrange("p (g e) -> p g e", g=GROUPS),
                             el[:, i, :].rearrange("p (g e) -> p g e", g=GROUPS),
                             ohg[:, i, :].unsqueeze(2).broadcast_to([TT, GROUPS, EPG]), ALU.add)
                step(ins)
                for k in range(TOPK):
                    step(dve.tensor_reduce(v5(4 + k), elm, AX, ALU.max))
                    step(tt(key, elm, over(v5(4 + k), NE), ALU.is_equal))
                    step(tt(key, key, ranks(NE), ALU.mult))
                    step(dve.tensor_reduce(s10[:, 0, k * NT:(k + 1) * NT], key, AX, ALU.max))
                    step(tt(oh[:, k], over(s10[:, 0, k * NT:(k + 1) * NT], NE), ranks(NE), ALU.is_equal))
                    if k == 0:
                        step(stt(elm, oh[:, k], -2.0 * BIG, elm, ALU.mult, ALU.add))
                tt(v5(7), v5(5), v5(4), ALU.subtract).then_inc(d_ok, 1)
                tt(picked[:, :, :], oh[:, 0], oh[:, 1], ALU.add).then_inc(pick_ok, 1)
                dve.wait_ge(e_ok, l + 1)
                step(tsc(v5(9), v5(8), 1.0, ALU.add))
                step(dve.reciprocal(v5(10), v5(9)))
                step(tt(wts[:, :NT], v5(3), v5(10), ALU.mult))
                step(tt(wts[:, NT:], wts[:, :NT], v5(8), ALU.mult))

                dve.wait_ge(rank_mm, l + 1)
                dve.tensor_copy(rank, ps[:TT, 7, :NT * NE].rearrange("p (i e) -> p i e", i=NT))
                step(dve.tensor_copy(cnt, ps[:TT, 7, NT * NE:(NT + 1) * NE]))
                step(tt(big8, cnt.unsqueeze(2).broadcast_to([TT, NE, MAXQ]),
                        thr[:, :].unsqueeze(1).broadcast_to([TT, NE, MAXQ]), ALU.is_gt))
                step(dve.tensor_reduce(nbl, big8, AX, ALU.add))
                step(dve.tensor_tensor_scan(cum, ones_f[:, :], nbl, 0.0, ALU.mult, ALU.add))
                step(tt(start, cum, nbl, ALU.subtract))

                def v10(k):
                    return s10[:, k, :]

                flat = rank.rearrange("p i e -> p (i e)").unsqueeze(1).broadcast_to([TT, TOPK, NT * NE])
                step(tt(prod, oh.rearrange("p k i e -> p k (i e)"), flat, ALU.mult))
                step(dve.tensor_reduce(v10(1), prod.rearrange("p k (i e) -> p (k i) e", e=NE), AX, ALU.add))
                ohv = oh.rearrange("p k i e -> p (k i) e")
                pv = prod.rearrange("p k (i e) -> p (k i) e", e=NE)
                step(tt(pv, ohv, start.unsqueeze(1).broadcast_to([TT, TOPK * NT, NE]), ALU.mult))
                step(dve.tensor_reduce(v10(2), pv, AX, ALU.add))
                step(tt(cmpq, v10(1).unsqueeze(2).broadcast_to([TT, TOPK * NT, MAXQ]),
                        thr[:, :].unsqueeze(1).broadcast_to([TT, TOPK * NT, MAXQ]), ALU.is_ge))
                step(dve.tensor_reduce(v10(3), cmpq, AX, ALU.add))
                step(stt(v10(4), v10(3), -float(ROWS), v10(1), ALU.mult, ALU.add))
                step(tsc(v10(5), v10(0), -1.0, ALU.mult, float(NE), ALU.add))
                step(tsc(v10(6), v10(3), 1.0, ALU.is_ge))
                step(stt(v10(7), v10(2), float(NE - 1), v10(3), ALU.add, ALU.add))
                step(tt(v10(7), v10(7), v10(5), ALU.subtract))
                step(tt(v10(7), v10(7), v10(6), ALU.mult))
                step(tt(v10(7), v10(7), v10(5), ALU.add))
                step(stt(slot_i[:, :], v10(7), float(ROWS), v10(4), ALU.mult, ALU.add))
                step(tt(rowhot, v10(4).unsqueeze(2).broadcast_to([TT, TOPK * NT, ROWS]),
                        iota[:, :ROWS].unsqueeze(1).broadcast_to([TT, TOPK * NT, ROWS]), ALU.is_equal))
                step(tt(blkhot, v10(7).unsqueeze(2).broadcast_to([TT, TOPK * NT, NBLK]),
                        iota[:, :NBLK].unsqueeze(1).broadcast_to([TT, TOPK * NT, NBLK]), ALU.is_equal))
                for k in range(TOPK):
                    b = blkhot[:, k * NT:(k + 1) * NT, :]
                    ins = tt(b, b, over(tokid[:, :], NBLK), ALU.mult)
                ins.then_inc(hot_ok, 1)
                dve.wait_ge(idx_mm, l + 1)
                dve.tensor_copy(idx[:, :], ps[:ROWS, 5, :NBLK]).then_inc(idx_ok[l], 1)
                step(tt(ovcmp, cum[0:1, :].unsqueeze(1).broadcast_to([1, OVER, NE]),
                        iota[0:1, :OVER].unsqueeze(2).broadcast_to([1, OVER, NE]), ALU.is_le))
                step(dve.tensor_reduce(s10[0:1, 8:12, :].rearrange("p a b -> p (a b)")[:, :OVER], ovcmp, AX, ALU.add))
                dve.tensor_copy(over_i[:, OVER:], cum[0:1, NE - 1:])
                tsc(over_i[:, :OVER], s10[0:1, 8:12, :].rearrange("p a b -> p (a b)")[:, :OVER], float(NE - 1),
                    ALU.min).then_inc(idx_ok[l], 1)

                def turned_rows(done, ready, v):
                    dve.wait_ge(done, v)
                    dve.tensor_copy(xgT, ps[:, 0, :KT * ROWS].rearrange("p (k t) -> p k t", k=KT)).then_inc(ready, 1)

                def hidden(ready):
                    tt(h, gated, ps[:, 1, FT * ROWS:2 * FT * ROWS], ALU.mult).then_inc(ready, 1)

                def expert(e, more=True):
                    dve.wait_ge(silu_ok[l], e + 1)
                    hidden(hid_ok[l])
                    if more:
                        turned_rows(t_mm[l], t_sb[l], e + 2)
                    dve.wait_ge(y_mm[l], e + 1)
                    dve.wait_ge(y_out[l], e * 16)
                    dve.tensor_copy(yo[:, 512:], ps[:ROWS, 3, :]).then_inc(y_dve[l], 1)

                turned_rows(t_mm[l], t_sb[l], 1)
                expert(0)
                with dve.Fori(0, TRIPS) as i:
                    for j in range(UNROLL):
                        expert(i * UNROLL + (PEEL + j))
                expert(NE - 1, more=False)
                n_over = dve.value_load(over_i[0:1, OVER:OVER + 1], min_val=0, max_val=OVER)
                with dve.If(n_over > 0):
                    dve.wait_ge(y_out[l], 16 * NE)
                    with dve.Fori(0, n_over) as o:
                        turned_rows(v_tmm[l], v_tsb[l], o + 1)
                        dve.wait_ge(v_silu[l], o + 1)
                        hidden(v_hid[l])
                        dve.wait_ge(v_y[l], o + 2)
                        dve.tensor_copy(yo[:, 512:], ps[:ROWS, 3, :]).then_inc(v_yd[l], 1)
                        dve.wait_ge(v_out[l], o * 16 + 16)
                    dve.memset(s5[:, 15, :], 0.0).then_inc(over_done[l], 1)
                dve.nop()

                q = 2 * l + 1
                for i in range(NT):
                    free_tile(q, i, l == 0)
                    z = zt[i % 2]
                    dve.wait_ge(pick_in[2 * l + i % 2], 32 * (i // 2 + 1))
                    step(tsc(z, r1[i % 2], wts[:, i:i + 1], ALU.mult))
                    step(stt(z, r2[i % 2], wts[:, NT + i:NT + i + 1], z, ALU.mult, ALU.add))
                    dve.wait_ge(res_in[2 * q + i % 2], residual_target(q, i))
                    stt(z, res[i % 2], ALPHA, z, ALU.mult, ALU.add).then_inc(z_done[q], 1)
                    norm(q, i)


_OUTS = [(1, SEQ, D), (DEC, 1, D), (1, 1, WA - 1, D), (1, DEC, WA - 1, D), (1, 1, WB - 1, D),
         (1, DEC, WB - 1, D), (1, 1, D), (1, DEC, D)]


def kernel(**inputs):
    import numpy as np
    import concourse.bacc as bacc
    from concourse.bass_utils import run_bass_kernel_spmd

    nc = bacc.Bacc("TRN2", target_bir_lowering=False, num_devices=1)
    arrays, args = {}, {}
    for name in inputs:
        x = np.ascontiguousarray(inputs[name])
        arrays[f"in_{name}"] = x
        args[name] = nc.dram_tensor(f"in_{name}", x.shape, mybir.dt.from_np(x.dtype), kind="ExternalInput").ap()
    outs = [nc.dram_tensor(f"out_{i}", list(s), F32, kind="ExternalOutput").ap() for i, s in enumerate(_OUTS)]
    build(nc, args, outs)
    r = run_bass_kernel_spmd(nc, [arrays], core_ids=[0])
    return tuple(r.results[0][f"out_{i}"] for i in range(len(_OUTS)))
```

```python
from contextlib import ExitStack

import concourse.bass as bass
from concourse import mybir

F32 = mybir.dt.float32
BF16 = mybir.dt.bfloat16
I32 = mybir.dt.int32
ALU = mybir.AluOpType
ACT = mybir.ActivationFunctionType
AX = mybir.AxisListType.X

P = 128
D = 1024
KT = D // P
SEQ = 512
DEC = 8
T = SEQ + DEC
TT = 104
NT = T // TT
LAST = SEQ - (NT - 1) * TT
HALF = T // 2
DEPTH = 2
ALPHA = (2.0 * DEPTH) ** 0.25
LN_EPS = 1e-5
RG_C = 8.0
GELU_C = 0.7978845608028654
GELU_A = 0.044715
GROUPS = 4
EPG = 8
NE = GROUPS * EPG
TOPK = 2
FE = 512
FT = FE // P
FH = FE // 2
ROWS = 64
CAP = 48
OVER = T * TOPK // CAP
NBLK = NE + OVER
MAXQ = -(-T // CAP) - 1
RING = 9
SLOT = KT * FE
BIG = 1.0e30

WA, WB = 3, 4
R_SA = 0
R_WA = R_SA + DEC * (WA - 1)
R_SB = R_WA + WA
R_H = R_SB + DEC * (WB - 1)
R_WB = R_H + DEC
R_BB = R_WB + WB
R_GA = R_BB + 1
R_GX = R_GA + 1
R_LAM = R_GX + 1
NROW = R_LAM + 1

U_IN = (KT, KT // 2 + 1)
U_OUT = 2
POS_IN = (0, U_IN[0] + U_OUT + 3 * NE)
POS_OUT = (POS_IN[0] + U_IN[0], POS_IN[1] + U_IN[1])
POS_EXP = (POS_OUT[0] + U_OUT, POS_OUT[1] + U_OUT)
UNROLL = 3
HEAD = UNROLL
TRIPS = (NE - HEAD - 1) // UNROLL
TAIL = range(HEAD + TRIPS * UNROLL, NE)


def ring_slot(pos):
    return pos % RING


def unit_dmas(pos):
    if pos < U_IN[0]:
        return 3
    return 2 if POS_IN[1] <= pos < POS_OUT[1] else 1


def load_target(pos):
    return sum(16 * unit_dmas(p) for p in range(pos % RING, pos + 1, RING))


def residual_target(q, i):
    return 16 * (i // 2 + 1) + (16 if q == 0 and i == NT - 1 else 0)


def z_buffers(q):
    return 2 if q % 2 == 0 else 4


def tiles_of(q, j):
    return len(range(j, NT, z_buffers(q)))


def x_out_target(q, i):
    n = z_buffers(q)
    return 16 * (tiles_of(q, i % n) * (q // 2) + i // n + 1) + (16 if q == 2 * DEPTH - 1 and i == NT - 1 else 0)


def rows_target(l, j, n):
    return 32 * (l * len(range(j, NE, UNROLL)) + n)


def build(nc, a, outs):
    y_prompt, y_sample, na_p, na_s, nb_p, nb_s, nh_p, nh_s = outs
    with ExitStack() as ctx:
        def sb(name, shape, dt=F32):
            return ctx.enter_context(nc.sbuf_tensor(name, shape, dt))

        def sem(name):
            return ctx.enter_context(nc.semaphore(name))

        def sems(name, n):
            return [sem(f"{name}{i}") for i in range(n)]

        x1_dram = [nc.dram_tensor(f"x1_{l}", [T, D], F32).ap() for l in range(DEPTH)]
        x2_dram = nc.dram_tensor("x2_0", [T, D], F32).ap()
        rows_dram = nc.dram_tensor("yrows", [NBLK * CAP, D], F32).ap()

        ring = sb("ring", [P, RING, SLOT])
        A = sb("A", [P, KT * T])
        Bt = sb("Bt", [P, KT * T])
        C = sb("C", [P, 6 * D])
        feat = sb("feat", [P, KT, NROW])
        wr = sb("wr", [P, KT, GROUPS + NE])
        ident = sb("ident", [P, P])
        conv0 = sb("conv0", [P, DEPTH, KT, DEC])
        spx = sb("spx", [P, 6, KT])
        new_cols = sb("new_cols", [P, KT, 20])
        before = sb("before", [TT, TT], BF16)
        ones = sb("ones", [TT, TT], BF16)
        iota = sb("iota", [TT, max(CAP, NBLK)])
        thr = sb("thr", [TT, MAXQ])
        tokid = sb("tokid", [TT, NT])
        rev = sb("rev", [TT, NE])
        ones_f = sb("ones_f", [TT, NE])
        unused = sb("unused", [TT, DEPTH])
        half_neg = sb("half_neg", [TT, 1])
        wts = sb("wts", [TT, TOPK * NT])
        slot_i = sb("slot_i", [TT, TOPK * NT], I32)
        idx = sb("idx", [CAP, NBLK], I32)
        cur = sb("cur", [CAP, 1], I32)
        over_i = sb("over_i", [1, OVER + 1], I32)
        stat = sb("stat", [TT, 2, 16])

        ps = ctx.enter_context(nc.psum_tensor("ps", [P, 8, 512], F32))

        xT = A[:, :].rearrange("p (k t) -> p k t", k=KT)
        hT = Bt[:, :].rearrange("p (k t) -> p k t", k=KT)
        xtok = C[:TT, 0:NT * D].rearrange("p (i d) -> p i d", i=NT)
        rowt = Bt[:NROW, 0:D]
        tmp = [C[:, i * T:(i + 1) * T] for i in range(9)]
        pad = C[:, 9 * T:10 * T + WB - 1]
        zero = Bt[:, 3 * D:4 * D]
        gain, shift = C[:TT, 0:D], C[:TT, D:2 * D]
        z_all = [C[:TT, (2 + i) * D:(3 + i) * D] for i in range(2)] + [Bt[:TT, i * D:(i + 1) * D] for i in range(2)]
        res = [C[:TT, (4 + i) * D:(5 + i) * D] for i in range(2)]
        r2 = [Bt[:TT, (2 + i) * D:(3 + i) * D] for i in range(2)]

        def zt(q, i):
            return z_all[i % z_buffers(q)]

        x1T = [A[:, i * 832:(i + 1) * 832].rearrange("p (k t) -> p k t", k=KT) for i in range(2)]
        new_rows = A[:20, 2048:2048 + D]
        rt = [0]

        def route(shape):
            n = 1
            for s in shape[1:]:
                n *= s
            v = Bt[:shape[0], rt[0]:rt[0] + n]
            rt[0] += n
            if len(shape) == 3:
                v = v.rearrange("p (a b) -> p a b", a=shape[1])
            if len(shape) == 4:
                v = v.rearrange("p (a b c) -> p a b c", a=shape[1], b=shape[2])
            return v

        lg = route([TT, NT, GROUPS + NE])
        gsh = route([TT, NT, GROUPS])
        gex = route([TT, NT, GROUPS])
        ohg = route([TT, NT, GROUPS])
        elm = route([TT, NT, NE])
        key = route([TT, NT, NE])
        oh = route([TT, TOPK, NT, NE])
        s5 = route([TT, 16, NT])
        rank = route([TT, NT, NE])
        cnt = route([TT, NE])
        nbl = route([TT, NE])
        cum = route([TT, NE])
        start = route([TT, NE])
        s10 = route([TT, 12, TOPK * NT])
        cmpq = route([TT, TOPK * NT, MAXQ])
        rowhot = route([TT, TOPK * NT, CAP])
        blkhot = route([TT, TOPK * NT, NBLK])
        big8 = route([TT, NE, MAXQ])
        prod = route([TT, TOPK, NT * NE])
        ovcmp = Bt[0:1, 0:OVER * NE].rearrange("p (a b) -> p a b", a=OVER)
        picked = sb("picked", [TT, NT, NE], BF16)
        assert rt[0] <= KT * T, rt[0]
        xg = [A[:ROWS, i * D:(i + 1) * D] for i in range(UNROLL)]
        xgT = A[:, 3 * D:3 * D + KT * ROWS].rearrange("p (k t) -> p k t", k=KT)
        gated = Bt[:, 0:FH]
        h = Bt[:, FH:2 * FH]
        hidT = Bt[:, 2 * FH:2 * FH + FT * ROWS]
        yo = [Bt[:, D + i * 512:D + (i + 1) * 512] for i in range(UNROLL)]

        x_in = sems("x_in", NT)
        row_in = sem("row_in")
        wr_in = sem("wr_in")
        zero_ok = sem("zero_ok")
        zero_out = sem("zero_out")
        pool_c = sem("pool_c")
        consts = sem("consts")
        dve_c = sem("dve_c")
        act_c = sem("act_c")
        setup_mm = sem("setup_mm")
        setup_dve = sem("setup_dve")
        setup_act = sem("setup_act")
        loaded = sems("loaded", RING)
        freed = sem("freed")
        L = range(DEPTH)
        mm_in = [sem(f"mm_in{l}") for l in L]
        mm_gate = sem("mm_gate")
        ev_a = [sem(f"ev_a{l}") for l in L]
        ev_b = [sem(f"ev_b{l}") for l in L]
        h_done = [sem(f"h_done{l}") for l in L]
        xc_done = sem("xc_done")
        lam_ok = sem("lam_ok")
        pad_ok = sem("pad_ok")
        sig_ok = sem("sig_ok")
        decay_ok = sem("decay_ok")
        gelu_in = sem("gelu_in")
        gelu_ok = sem("gelu_ok")
        sq_in = sem("sq_in")
        sq_ok = sem("sq_ok")
        st_mm = sem("st_mm")
        st_sb = sem("st_sb")
        out_mm = sem("out_mm")
        par_in = sem("par_in")
        res_in = [sem(f"res_in{l}_{j}") for l in range(2 * DEPTH) for j in range(2)]
        z_done = [sem(f"z_done{l}") for l in range(2 * DEPTH)]
        var_ok = [sem(f"var_ok{l}") for l in range(2 * DEPTH)]
        rstd_ok = [sem(f"rstd_ok{l}") for l in range(2 * DEPTH)]
        x_done = [sem(f"x_done{l}") for l in range(2 * DEPTH)]
        x_outs = [sems("x_out_mixer", 2), sems("x_out_moe", 4)]
        scaled = sem("scaled")
        turned = [sem(f"turned{l}") for l in range(3)]
        turned_sb = [sem(f"turned_sb{l}") for l in range(3)]
        logit_mm = sem("logit_mm")
        gsh_ok = sem("gsh_ok")
        gex_ok = sem("gex_ok")
        d_ok = sem("d_ok")
        e_ok = sem("e_ok")
        pick_ok = sem("pick_ok")
        rank_mm = sem("rank_mm")
        hot_ok = sem("hot_ok")
        idx_mm = sem("idx_mm")
        idx_ok = [sem(f"idx_ok{l}") for l in L]
        over_done = [sem(f"over_done{l}") for l in L]
        gath = [sem(f"gath{l}_{j}") for l in L for j in range(UNROLL)]
        t_mm = [sem(f"t_mm{l}") for l in L]
        t_sb = [sem(f"t_sb{l}") for l in L]
        gu_mm = [sem(f"gu_mm{l}") for l in L]
        silu_ok = [sem(f"silu_ok{l}") for l in L]
        hid_ok = [sem(f"hid_ok{l}") for l in L]
        y_mm = [sem(f"y_mm{l}") for l in L]
        y_act = [sem(f"y_act{l}") for l in L]
        h_mm = [sem(f"h_mm{l}") for l in L]
        h_sb = [sem(f"h_sb{l}") for l in L]
        y_out = sems("y_out", UNROLL)
        v_cur = [sem(f"v_cur{l}") for l in L]
        v_load = [sem(f"v_load{l}") for l in L]
        v_gath = [sem(f"v_gath{l}") for l in L]
        v_tmm = [sem(f"v_tmm{l}") for l in L]
        v_tsb = [sem(f"v_tsb{l}") for l in L]
        v_gu = [sem(f"v_gu{l}") for l in L]
        v_silu = [sem(f"v_silu{l}") for l in L]
        v_hid = [sem(f"v_hid{l}") for l in L]
        v_y = [sem(f"v_y{l}") for l in L]
        v_ya = [sem(f"v_ya{l}") for l in L]
        v_hmm = [sem(f"v_hmm{l}") for l in L]
        v_hsb = [sem(f"v_hsb{l}") for l in L]
        v_out = [sem(f"v_out{l}") for l in L]
        pick_in = [sem(f"pick_in{l}_{j}") for l in L for j in range(2)]
        state_out = sem("state_out")

        w_in0 = a["a_w_in"][0].rearrange("(p k) (j m q) -> p k j m q", k=KT, j=3, m=KT)
        w_in1 = a["b_w_in"][0].rearrange("(p k) (j m q) -> p k j m q", k=KT, j=2, m=KT // 2)
        w_out = [w[0].rearrange("(k p) n -> p k n", p=P) for w in (a["a_w_out"], a["b_w_out"])]
        w_ga = a["b_gate_a_w"][0].rearrange("n p j -> p n j")
        w_gx = a["b_gate_x_w"][0].rearrange("n p j -> p n j")
        gates = [a["moe_w_gate"][l].rearrange("e (p k) f -> e p (k f)", k=KT) for l in L]
        ups = [a["moe_w_up"][l].rearrange("e (p k) f -> e p (k f)", k=KT) for l in L]
        downs = [a["moe_w_down"][l].rearrange("e (m p) n -> e p m n", p=P) for l in L]

        def prompt_rows(i):
            return TT if i < NT - 1 else LAST

        def x_out(q, i):
            return x_outs[q % 2][i % z_buffers(q)]

        def all_out(engine, q):
            for j in range(z_buffers(q)):
                last = max(range(j, NT, z_buffers(q)))
                engine.wait_ge(x_out(q, j), x_out_target(q, last))

        def all_rows_out(engine, l):
            for j in range(UNROLL):
                engine.wait_ge(y_out[j], rows_target(l + 1, j, 0))

        block = ctx.enter_context(nc.Block())

        @block.sync
        def _(sp):
            def room(pos, off=0):
                if pos >= RING:
                    sp.wait_ge(freed, pos - RING + 1 + off)

            def expert(l, pos, e, off=0):
                for u, w in enumerate((gates, ups, downs)):
                    room(pos + u, off)
                    s = ring_slot(pos + u)
                    out = ring[:, s, :] if u < 2 else ring[:, s, :].rearrange("p (m n) -> p m n", m=FT)
                    sp.dma_start(out, w[l][e]).then_inc(loaded[s], 16)

            def input_unit0(c):
                for j in range(3):
                    out = ring[:, ring_slot(c), :KT * 3 * P].rearrange("p (k j q) -> p k j q", k=KT, j=3)
                    sp.dma_start(out[:, :, j, :], w_in0[:, :, j, c, :]).then_inc(loaded[ring_slot(c)], 16)

            def input_unit1(m):
                pos = POS_IN[1] + m
                room(pos)
                for j in range(2):
                    out = ring[:, ring_slot(pos), :].rearrange("p (k j q) -> p k j q", k=KT, j=2)
                    sp.dma_start(out[:, :, j, :], w_in1[:, :, j, m, :]).then_inc(loaded[ring_slot(pos)], 16)

            for i in range(NT):
                n = prompt_rows(i)
                sp.dma_start(xtok[:n, i, :], a["x_prompt"][0, i * TT:i * TT + n, :]).then_inc(x_in[i], 16)
            sp.dma_start(xtok[LAST:TT, NT - 1, :], a["x_sample"][:, 0, :]).then_inc(x_in[NT - 1], 16)
            for l in L:
                if l == 0:
                    for c in range(KT):
                        input_unit0(c)
                else:
                    for m in range(KT // 2):
                        if m == 2:
                            all_out(sp, 1)
                        input_unit1(m)
                    pos = POS_IN[1] + KT // 2
                    room(pos)
                    for j, w in enumerate((w_ga, w_gx)):
                        out = ring[:, ring_slot(pos), j * D:(j + 1) * D].rearrange("p (n q) -> p n q", n=KT)
                        sp.dma_start(out, w).then_inc(loaded[ring_slot(pos)], 16)
                for u in range(U_OUT):
                    pos = POS_OUT[l] + u
                    room(pos)
                    out = ring[:, ring_slot(pos), :].rearrange("p (k n) -> p k n", k=KT)
                    sp.dma_start(out, w_out[l][:, :, u * 512:(u + 1) * 512]).then_inc(loaded[ring_slot(pos)], 16)
                for e in range(HEAD):
                    expert(l, POS_EXP[l] + 3 * e, e)
                with sp.Fori(0, TRIPS) as i:
                    for j in range(UNROLL):
                        expert(l, POS_EXP[l] + 3 * (HEAD + j), i * UNROLL + (HEAD + j), i * (3 * UNROLL))
                for e in TAIL:
                    expert(l, POS_EXP[l] + 3 * e, e)
                sp.wait_ge(idx_ok[l], 2)
                n_over = sp.value_load(over_i[0:1, OVER:OVER + 1], min_val=0, max_val=OVER)
                with sp.If(n_over > 0):
                    sp.wait_ge(y_mm[l], NE)
                    with sp.Fori(0, n_over) as o:
                        sp.wait_ge(v_y[l], o + 1)
                        e = sp.value_load(over_i[0:1, bass.ds(o, 1)], min_val=0, max_val=NE - 1)
                        for u, w in enumerate((gates, ups, downs)):
                            out = ring[:, u, :] if u < 2 else ring[:, u, :].rearrange("p (m n) -> p m n", m=FT)
                            sp.dma_start(out, w[l][e]).then_inc(v_load[l], 16)
                    sp.wait_ge(over_done[l], 1)
                sp.nop()

        @block.gpsimd
        def _(pool):
            n = [0]

            def step(ins):
                n[0] += 1
                ins.then_inc(pool_c, 1)
                pool.wait_ge(pool_c, n[0])

            step(pool.memset(ident[:, :], 0.0))
            pool.memset(zero, 0.0).then_inc(zero_ok, 1)
            step(pool.memset(before[:, :], 1.0))
            pool.affine_select(out=ident[:, :], in_=ident[:, :], compare_op=ALU.not_equal, fill=1.0,
                               base=0, pattern=[[-1, P]], channel_multiplier=1).then_inc(consts, 1)
            pool.affine_select(out=before[:, :], in_=before[:, :], compare_op=ALU.is_gt, fill=0.0,
                               base=0, pattern=[[1, TT]], channel_multiplier=-1).then_inc(consts, 1)
            pool.memset(ones[:, :], 1.0).then_inc(consts, 1)
            pool.memset(half_neg[:, :], -0.5).then_inc(consts, 1)
            pool.memset(ones_f[:, :], 1.0).then_inc(consts, 1)
            pool.iota(iota[:, :], pattern=[[1, max(CAP, NBLK)]], base=0, channel_multiplier=0,
                      allow_small_or_imprecise_dtypes=True).then_inc(consts, 1)
            pool.iota(thr[:, :], pattern=[[CAP, MAXQ]], base=CAP, channel_multiplier=0,
                      allow_small_or_imprecise_dtypes=True).then_inc(consts, 1)
            pool.iota(tokid[:, :], pattern=[[TT, NT]], base=0, channel_multiplier=1,
                      allow_small_or_imprecise_dtypes=True).then_inc(consts, 1)
            pool.iota(rev[:, :], pattern=[[-1, NE]], base=NE, channel_multiplier=0,
                      allow_small_or_imprecise_dtypes=True).then_inc(consts, 1)

            pool.wait_ge(consts, 9)

            def root(q, i):
                pool.wait_ge(var_ok[q], i + 1)
                st = stat[:, i % 2, :]
                pool.tensor_tensor(st[:, 15:16], st[:, 14:15], half_neg[:, :], ALU.pow).then_inc(rstd_ok[q], 1)

            for l in L:
                for i in range(NT):
                    root(2 * l, i)
                all_out(pool, 2 * l)
                pool.wait_ge(logit_mm, NT * (l + 1))
                step(pool.memset(A[CAP // 32 * 32:ROWS, 0:UNROLL * D], 0.0))
                pool.wait_ge(idx_ok[l], 1)
                for e in range(NE):
                    if e >= UNROLL:
                        pool.wait_ge(t_mm[l], e - UNROLL + 1)
                    pool.indirect_dma_start(
                        out=xg[e % UNROLL][:CAP], out_offset=None, in_=x1_dram[l],
                        in_offset=bass.IndirectOffsetOnAxis(ap=idx[:, e:e + 1], axis=0),
                    ).then_inc(gath[UNROLL * l + e % UNROLL], 16)
                pool.wait_ge(idx_ok[l], 2)
                n_over = pool.value_load(over_i[0:1, OVER:OVER + 1], min_val=0, max_val=OVER)
                with pool.If(n_over > 0):
                    pool.wait_ge(t_mm[l], NE)
                    with pool.Fori(0, n_over) as o:
                        pool.tensor_copy(cur[:, 0:1], idx[:, bass.ds(o + NE, 1)]).then_inc(v_cur[l], 1)
                        pool.wait_ge(v_cur[l], o * 2 + 1)
                        pool.tensor_tensor(unused[:, l:l + 1], half_neg[:, :], half_neg[:, :],
                                           ALU.mult).then_inc(v_cur[l], 1)
                        pool.indirect_dma_start(
                            out=xg[0][:CAP], out_offset=None, in_=x1_dram[l],
                            in_offset=bass.IndirectOffsetOnAxis(ap=cur[:, 0:1], axis=0),
                        ).then_inc(v_gath[l], 16)
                        pool.wait_ge(v_y[l], o + 2)
                    pool.wait_ge(over_done[l], 1)
                pool.nop()
                all_rows_out(pool, l)
                q = 2 * l + 1
                for i in range(NT + 1):
                    if i < NT:
                        if i >= 2:
                            pool.wait_ge(z_done[q], i - 1)
                        if i >= z_buffers(q):
                            pool.wait_ge(x_out(q, i), x_out_target(q, i - z_buffers(q)))
                            if l == 0:
                                pool.wait_ge(turned[1], i - z_buffers(q) + 1)
                        for k, r in enumerate((zt(q, i), r2[i % 2])):
                            c = k * NT + i
                            pool.indirect_dma_start(
                                out=r, out_offset=None, in_=rows_dram,
                                in_offset=bass.IndirectOffsetOnAxis(ap=slot_i[:, c:c + 1], axis=0),
                            ).then_inc(pick_in[2 * l + i % 2], 16)
                    if i >= 1:
                        root(q, i - 1)

        @block.tensor
        def _(pe):
            def product(bank, lhs, rhs, first=False):
                for k in range(KT):
                    mm = pe.matmul(bank, lhs(k), rhs(k), start=(k == 0), stop=(k == KT - 1))
                    if k == 0 and first:
                        mm.then_inc(freed, 1)
                return mm

            def turn_tile(x, bank0):
                xv = x.rearrange("r (p k) -> r k p", k=KT)
                for k in range(KT):
                    mm = pe.transpose(ps[:, bank0 + k // 4, (k % 4) * TT:(k % 4 + 1) * TT], xv[:, k, :],
                                      ident[:TT, :TT])
                return mm

            pe.wait_ge(consts, 1)
            for i in range(NT):
                pe.wait_ge(x_in[i], 16 if i < NT - 1 else 32)
                if i >= 4:
                    pe.wait_ge(setup_dve, i - 3)
                    pe.wait_ge(setup_act, i - 3)
                turn_tile(xtok[:, i, :], 2 * (i % 4)).then_inc(setup_mm, 1)
            pe.wait_ge(setup_dve, NT)
            pe.wait_ge(setup_act, NT)

            for c in range(KT):
                s = ring_slot(c)
                pe.wait_ge(loaded[s], load_target(c))
                for jj, j in enumerate((1, 2, 0)):
                    n = 3 * c + jj
                    if n >= 4:
                        pe.wait_ge((ev_a[0], ev_b[0], h_done[0])[(n - 4) % 3], (n - 4) // 3 + 1)
                    for hf in range(2):
                        mm = product(ps[:, 2 * (n % 4) + hf, :HALF],
                                     lambda k: ring[:, s, (k * 3 + j) * P:(k * 3 + j + 1) * P],
                                     lambda k: xT[:, k, hf * HALF:(hf + 1) * HALF],
                                     first=(c > 0 and jj == 0 and hf == 0))
                    mm.then_inc(mm_in[0], 1)
                    if n == 0:
                        pe.wait_ge(row_in, 16 * 9)
                        for r in range(KT):
                            mm = pe.transpose(ps[:, 7, r * NROW:(r + 1) * NROW], rowt[:, r * P:(r + 1) * P],
                                              ident[:NROW, :NROW])
                        mm.then_inc(setup_mm, 1)
                    if n == 2:
                        pe.wait_ge(setup_dve, NT + 1)

            def input_product(c, jj, hf):
                pos = POS_IN[1] + c // 2
                s = ring_slot(pos)
                pe.wait_ge(loaded[s], load_target(pos))
                col = (1 - jj) * 2 * P + (c % 2) * P
                return product(ps[:, 2 * jj + hf, :HALF],
                               lambda k: ring[:, s, k * FE + col:k * FE + col + P],
                               lambda k: xT[:, k, hf * HALF:(hf + 1) * HALF],
                               first=(c % 2 == 0 and jj == 0 and hf == 0))

            EARLY = KT - 2

            def out_part(l, i, lo, hi, first=False):
                ends = []
                for nh in range(2):
                    s = ring_slot(POS_OUT[l] + nh)
                    if i == 0:
                        pe.wait_ge(loaded[s], load_target(POS_OUT[l] + nh))
                    for k in range(lo, hi):
                        mm = pe.matmul(ps[:TT, 2 * (i % 2) + nh, :], hT[:, k, i * TT:(i + 1) * TT],
                                       ring[:, s, k * 512:(k + 1) * 512], start=(k == 0), stop=(k == KT - 1))
                        if first and nh == 0 and k == lo:
                            mm.then_inc(freed, 1)
                    ends.append(mm)
                return ends

            for l in L:
                if l == 1:
                    def rg_gates(c):
                        s = ring_slot(POS_IN[1] + KT // 2)
                        pe.wait_ge(xc_done, c + 1)
                        if c == 0:
                            pe.wait_ge(loaded[s], load_target(POS_IN[1] + KT // 2))
                        else:
                            pe.wait_ge(sig_ok, 2 * c)
                        for g in range(2):
                            for hf in range(2):
                                mm = pe.matmul(ps[:, 4 + 2 * g + hf, :HALF],
                                               ring[:, s, g * D + c * P:g * D + (c + 1) * P],
                                               tmp[6 + c % 2][:, hf * HALF:(hf + 1) * HALF],
                                               start=True, stop=True)
                                if c == KT - 1 and g == 0 and hf == 0:
                                    mm.then_inc(freed, 1)
                            mm.then_inc(mm_gate, 1)

                    pe.wait_ge(turned_sb[1], NT)
                    for c in range(KT):
                        for jj in range(2):
                            if c >= 1:
                                pe.wait_ge((ev_a[1], ev_b[1])[jj], c)
                                input_product(c, jj, 0)
                            input_product(c, jj, 1).then_inc(mm_in[1], 1)
                        if c >= 1:
                            rg_gates(c - 1)
                pe.wait_ge(h_done[l], KT - 1 if l == 0 else EARLY)
                if l == 1:
                    pe.wait_ge(ev_a[1], KT)
                out_part(l, 0, 0, EARLY, first=(l == 0))
                if l == 1:
                    rg_gates(KT - 1)
                pe.wait_ge((ev_a[0], ev_b[1])[l], KT)
                out_part(l, 1, 0, EARLY, first=(l == 1))

                q = 2 * l
                n_new = (10, 20)[l]

                def turn(i):
                    pe.wait_ge(x_done[q], i + 1)
                    if i >= 1:
                        pe.wait_ge(turned_sb[q], i)
                    turn_tile(zt(q, i), 4).then_inc(turned[q], 1)

                def logits(i):
                    pe.wait_ge(turned_sb[q], i + 1)
                    for k in range(KT):
                        mm = pe.matmul(ps[:TT, 6, i * (GROUPS + NE):(i + 1) * (GROUPS + NE)],
                                       x1T[i % 2][:, k, :], wr[:, k, :], start=(k == 0), stop=(k == KT - 1))
                    mm.then_inc(logit_mm, 1)

                pe.wait_ge(h_done[l], KT)
                for i in range(NT):
                    if i >= 2:
                        pe.wait_ge(z_done[q], i - 1)
                    ends = out_part(l, i, EARLY if i < 2 else 0, KT)
                    if i == NT - 1:
                        ends[0].then_inc(freed, 1)
                    ends[1].then_inc(out_mm, 1)
                    if i == 0:
                        for c in range(KT):
                            mm = pe.transpose(ps[:n_new, 6 + c // 4, (c % 4) * P:(c % 4 + 1) * P],
                                              new_cols[:, c, :n_new], ident[:, :])
                        mm.then_inc(st_mm, 1)
                    if i >= 1:
                        turn(i - 1)
                    if i == 2:
                        pe.wait_ge(st_sb, l + 1)
                        pe.wait_ge(wr_in, 32 * (l + 1))
                    if i >= 2:
                        logits(i - 2)
                logits(NT - 2)
                turn(NT - 1)
                logits(NT - 1)

                pe.wait_ge(pick_ok, l + 1)
                pe.wait_ge(consts, 9)
                for i in range(NT):
                    for j in range(i + 1):
                        pe.matmul(ps[:TT, 7, i * NE:(i + 1) * NE], (ones if j < i else before)[:, :],
                                  picked[:, j, :], start=(j == 0), stop=(j == i))
                for j in range(NT):
                    mm = pe.matmul(ps[:TT, 7, NT * NE:(NT + 1) * NE], ones[:, :], picked[:, j, :],
                                   start=(j == 0), stop=(j == NT - 1))
                mm.then_inc(rank_mm, 1)
                pe.wait_ge(hot_ok, l + 1)
                for c in range(TOPK * NT):
                    mm = pe.matmul(ps[:CAP, 5, :NBLK], rowhot[:, c, :], blkhot[:, c, :],
                                   start=(c == 0), stop=(c == TOPK * NT - 1))
                mm.then_inc(idx_mm, 1)

                def turn_rows(x, done, free=False):
                    xv = x.rearrange("r (p k) -> r k p", k=KT)
                    for k in range(KT):
                        mm = pe.transpose(ps[:, 0, k * ROWS:(k + 1) * ROWS], xv[:, k, :], ident[:ROWS, :ROWS])
                        if free and k == 0:
                            mm.then_inc(freed, 1)
                    mm.then_inc(done, 1)

                def gate_up(slots, done, free):
                    for u in range(2):
                        for k in range(KT):
                            for hf in range(2):
                                col = k * FE + hf * FH
                                mm = pe.matmul(ps[hf * ROWS:(hf + 1) * ROWS, 1, u * FH:(u + 1) * FH],
                                               xgT[:, k, :], ring[:, slots[u], col:col + FH],
                                               start=(k == 0), stop=(k == KT - 1))
                                if free and u == 0 and (k, hf) in ((0, 0), (KT - 1, 1)):
                                    mm.then_inc(freed, 1)
                    mm.then_inc(done, 1)

                def turn_hidden(done, free=False):
                    for c in range(2):
                        mm = pe.transpose(ps[:, 4, c * P:(c + 1) * P], h[:, c * P:(c + 1) * P], ident[:, :])
                        if free and c == 0:
                            mm.then_inc(freed, 1)
                    mm.then_inc(done, 1)

                def down(slot, done):
                    for m in range(FT):
                        at = (m % 2) * P + (m // 2) * ROWS
                        for nh in range(2):
                            mm = pe.matmul(ps[nh * ROWS:(nh + 1) * ROWS, 2, :], hidT[:, at:at + ROWS],
                                           ring[:, slot, m * D + nh * 512:m * D + (nh + 1) * 512],
                                           start=(m == 0), stop=(m == FT - 1))
                    mm.then_inc(done, 1)

                def expert(e, e0, trip=0, more=True):
                    pos = POS_EXP[l] + 3 * e0
                    slots = [ring_slot(pos + u) for u in range(3)]
                    pe.wait_ge(t_sb[l], e + 1)
                    for u in range(2):
                        pe.wait_ge(loaded[slots[u]], load_target(pos + u) + trip * 16)
                    b = (e0 + 1) % UNROLL
                    if more:
                        pe.wait_ge(gath[UNROLL * l + b], 16 * ((e0 + 1) // UNROLL + 1) + trip * 16)
                    gate_up(slots, gu_mm[l], True)
                    if more:
                        turn_rows(xg[b], t_mm[l], True)
                    pe.wait_ge(hid_ok[l], e + 1)
                    turn_hidden(h_mm[l], not more)
                    pe.wait_ge(loaded[slots[2]], load_target(pos + 2) + trip * 16)
                    pe.wait_ge(h_sb[l], e + 1)
                    pe.wait_ge(y_act[l], e)
                    down(slots[2], y_mm[l])

                pe.wait_ge(gath[UNROLL * l], 16)
                turn_rows(xg[0], t_mm[l])
                for e in range(HEAD):
                    expert(e, e)
                with pe.Fori(0, TRIPS) as i:
                    for j in range(UNROLL):
                        expert(i * UNROLL + (HEAD + j), HEAD + j, i)
                for e in TAIL:
                    expert(e, e, more=(e < NE - 1))
                pe.wait_ge(idx_ok[l], 2)
                n_over = pe.value_load(over_i[0:1, OVER:OVER + 1], min_val=0, max_val=OVER)
                with pe.If(n_over > 0):
                    pe.wait_ge(y_act[l], NE)
                    pe.matmul(ps[:ROWS, 1, :ROWS], ident[:, :ROWS], ident[:, :ROWS], start=True,
                              stop=True).then_inc(v_y[l], 1)
                    with pe.Fori(0, n_over) as o:
                        pe.wait_ge(v_gath[l], o * 16 + 16)
                        pe.matmul(ps[:ROWS, 1, :ROWS], ident[:, :ROWS], ident[:, :ROWS], start=True, stop=True)
                        turn_rows(xg[0], v_tmm[l])
                        pe.wait_ge(v_tsb[l], o + 1)
                        pe.wait_ge(v_load[l], o * 48 + 48)
                        gate_up((0, 1), v_gu[l], False)
                        pe.wait_ge(v_hid[l], o + 1)
                        turn_hidden(v_hmm[l])
                        pe.wait_ge(v_hsb[l], o + 1)
                        down(2, v_y[l])
                        pe.wait_ge(v_ya[l], o + 1)
                pe.nop()
                if l == 0:
                    for i in range(NT):
                        pe.wait_ge(x_done[1], i + 1)
                        if i >= 1:
                            pe.wait_ge(turned_sb[1], i)
                        turn_tile(zt(1, i), 4).then_inc(turned[1], 1)
                        if i in (2, 3):
                            pe.wait_ge(turned_sb[1], 3)
                            pe.wait_ge(y_act[0], NE)
                            input_product(0, i - 2, 0)

        @block.scalar
        def _(act):
            n = [0]

            def step(ins):
                n[0] += 1
                ins.then_inc(act_c, 1)
                act.wait_ge(act_c, n[0])

            def rows_in(r, k, src):
                act.dma_start(rowt[r:r + k, :], src).then_inc(row_in, 16)

            rows_in(R_SA, DEC * 2, a["state_conv_a"][0].rearrange("b w d -> (b w) d"))
            rows_in(R_WA, WA, a["a_conv_w"][0])
            rows_in(R_SB, DEC * 3, a["state_conv_b"][0].rearrange("b w d -> (b w) d"))
            rows_in(R_H, DEC, a["state_h"][0])
            rows_in(R_WB, WB, a["b_conv_w"][0])
            for r, name in ((R_BB, "b_conv_b"), (R_GA, "b_gate_a_b"), (R_GX, "b_gate_x_b"), (R_LAM, "b_lambda")):
                rows_in(r, 1, a[name])

            def router_weights(l):
                for name, lo, hi in (("moe_w_group", 0, GROUPS), ("moe_w_expert", GROUPS, GROUPS + NE)):
                    act.dma_start(wr[:, :, lo:hi],
                                  a[name][l].rearrange("(p k) g -> p k g", k=KT)).then_inc(wr_in, 16)

            router_weights(0)
            act.dma_start(na_s[0, :, 0, :], a["state_conv_a"][0, :, 1, :]).then_inc(state_out, 16)
            act.dma_start(nb_s[0, :, 0:2, :], a["state_conv_b"][0, :, 1:3, :]).then_inc(state_out, 16)

            for i in range(NT):
                act.wait_ge(setup_mm, i + 1)
                act.activation(xT[:, 4:8, i * TT:(i + 1) * TT],
                               ps[:, 2 * (i % 4) + 1, :4 * TT].rearrange("p (k t) -> p k t", k=4),
                               ACT.Copy).then_inc(setup_act, 1)
            act.wait_ge(lam_ok, 1)
            act.activation(spx[:, 2, :], spx[:, 1, :], ACT.Exp, scale=-1.0).then_inc(lam_ok, 1)

            def halves(v):
                return v.rearrange("p (a b) -> p a b", a=2)

            def banks(pair):
                return ps[:, 2 * pair:2 * pair + 2, :HALF]

            for c in range(KT):
                act.wait_ge(mm_in[0], 3 * c + 1)
                if c >= 2:
                    act.wait_ge(ev_b[0], c - 1)
                act.activation(halves(tmp[c % 2]), banks((3 * c) % 4), ACT.Copy).then_inc(ev_a[0], 1)
                if c == 1:
                    act.wait_ge(zero_ok, 1)
                    for i in range(NE * CAP, NBLK * CAP, P):
                        n = min(P, NBLK * CAP - i)
                        act.dma_start(rows_dram[i:i + n, :], zero[:n]).then_inc(zero_out, 16)

            for l in L:
                if l == 1:
                    def recurrence_gates(c):
                        act.wait_ge(mm_gate, 2 * c + 1)
                        if c >= 1:
                            act.wait_ge(h_done[1], c)
                        act.activation(halves(tmp[2]), banks(2), ACT.Sigmoid,
                                       bias=feat[:, c, R_GA:R_GA + 1]).then_inc(sig_ok, 1)
                        act.wait_ge(mm_gate, 2 * c + 2)
                        act.activation(halves(tmp[3]), banks(3), ACT.Sigmoid,
                                       bias=feat[:, c, R_GX:R_GX + 1]).then_inc(sig_ok, 1)
                        act.wait_ge(sig_ok, 2 * c + 2)
                        act.activation(tmp[4], tmp[2], ACT.Exp, scale=spx[:, 0, c:c + 1]).then_inc(decay_ok, 1)
                        act.activation(tmp[5], tmp[2], ACT.Tanh, scale=spx[:, 0, c:c + 1]).then_inc(decay_ok, 1)
                        act.wait_ge(gelu_in, c + 1)
                        act.activation(tmp[8], tmp[8], ACT.Tanh, scale=GELU_C).then_inc(gelu_ok, 1)
                        act.wait_ge(sq_in, c + 1)
                        act.activation(tmp[2], tmp[2], ACT.Sqrt).then_inc(sq_ok, 1)

                    act.wait_ge(lam_ok, 3)
                    for c in range(KT):
                        act.wait_ge(mm_in[1], 2 * c + 1)
                        act.wait_ge(xc_done, c) if c >= 1 else act.wait_ge(pad_ok, 2)
                        act.activation(pad[:, WB - 1:].rearrange("p (a b) -> p a b", a=2), banks(0),
                                       ACT.Copy).then_inc(ev_a[1], 1)
                        act.wait_ge(mm_in[1], 2 * c + 2)
                        if c >= 2:
                            act.wait_ge(h_done[1], c - 1)
                        act.activation(halves(tmp[c % 2]), banks(1), ACT.Copy).then_inc(ev_b[1], 1)
                        if c >= 1:
                            recurrence_gates(c - 1)
                    recurrence_gates(KT - 1)

                def norm_loads(q):
                    g, b = (a["ln1_g"], a["ln1_b"]) if q % 2 == 0 else (a["ln2_g"], a["ln2_b"])
                    act.dma_start(gain, g[q // 2:q // 2 + 1, :].broadcast_to([TT, D])).then_inc(par_in, 16)
                    act.dma_start(shift, b[q // 2:q // 2 + 1, :].broadcast_to([TT, D])).then_inc(par_in, 16)

                def residual(q, i):
                    if i >= 2:
                        act.wait_ge(z_done[q], i - 1)
                    n = prompt_rows(i)
                    if q == 0:
                        act.dma_start(res[i % 2][:n], a["x_prompt"][0, i * TT:i * TT + n, :]).then_inc(res_in[2 * q + i % 2], 16)
                        if n < TT:
                            act.dma_start(res[i % 2][n:], a["x_sample"][:, 0, :]).then_inc(res_in[2 * q + i % 2], 16)
                    else:
                        src = (None, x1_dram[0], x2_dram, x1_dram[1])[q]
                        act.dma_start(res[i % 2], src[i * TT:(i + 1) * TT, :]).then_inc(res_in[2 * q + i % 2], 16)

                q = 2 * l
                act.wait_ge(h_done[l], KT)
                if l == 1:
                    all_out(act, 1)
                norm_loads(q)
                residual(q, 0)
                residual(q, 1)

                act.wait_ge(st_mm, l + 1)
                n_new = (10, 20)[l]
                act.activation(new_rows[:n_new].rearrange("r (a b) -> r a b", a=2), ps[:n_new, 6:8, :],
                               ACT.Copy).then_inc(st_sb, 1)
                act.wait_ge(st_sb, l + 1)
                if l == 0:
                    act.dma_start(na_p[0, 0], new_rows[0:2]).then_inc(state_out, 16)
                    act.dma_start(na_s[0, :, 1, :], new_rows[2:10]).then_inc(state_out, 16)
                else:
                    act.dma_start(nb_p[0, 0], new_rows[0:3]).then_inc(state_out, 16)
                    act.dma_start(nb_s[0, :, 2, :], new_rows[3:11]).then_inc(state_out, 16)
                    act.dma_start(nh_p[0], new_rows[11:12]).then_inc(state_out, 16)
                    act.dma_start(nh_s[0], new_rows[12:20]).then_inc(state_out, 16)

                for i in range(NT):
                    act.wait_ge(x_done[q], i + 1)
                    act.dma_start(x1_dram[l][i * TT:(i + 1) * TT, :], zt(q, i)).then_inc(x_out(q, i), 16)
                    act.wait_ge(turned[q], i + 1)
                    if i >= 2:
                        act.wait_ge(logit_mm, NT * l + i - 1)
                    act.activation(x1T[i % 2].rearrange("p (a k) t -> p a (k t)", a=2), ps[:, 4:6, :4 * TT],
                                   ACT.Copy).then_inc(turned_sb[q], 1)
                    if i + 2 < NT:
                        residual(q, i + 2)

                act.wait_ge(gsh_ok, l + 1)
                act.activation(gex, gsh, ACT.Exp).then_inc(gex_ok, 1)
                act.wait_ge(d_ok, l + 1)
                act.activation(s5[:, 8, :], s5[:, 7, :], ACT.Exp).then_inc(e_ok, 1)

                q = 2 * l + 1
                all_out(act, 2 * l)
                norm_loads(q)
                residual(q, 0)
                residual(q, 1)
                if l == 0:
                    act.wait_ge(logit_mm, NT)
                    router_weights(1)

                act.wait_ge(idx_ok[l], 2)

                def rows_to_dram(row, rows, done):
                    for nh in range(2):
                        act.dma_start(rows_dram[bass.ds(row, CAP), nh * 512:(nh + 1) * 512],
                                      rows[nh * ROWS:nh * ROWS + CAP, :]).then_inc(done, 16)

                def expert(e, e0, trip=0):
                    act.wait_ge(gu_mm[l], e + 1)
                    act.wait_ge(hid_ok[l], e)
                    act.activation(gated, ps[:, 1, :FH], ACT.Silu).then_inc(silu_ok[l], 1)
                    act.wait_ge(y_mm[l], e + 1)
                    j = e0 % UNROLL
                    if e0 >= UNROLL:
                        act.wait_ge(y_out[j], rows_target(l, j, e0 // UNROLL) + trip * 32)
                    act.activation(yo[j], ps[:, 2, :], ACT.Copy).then_inc(y_act[l], 1)
                    act.wait_ge(y_act[l], e + 1)
                    rows_to_dram(e * CAP, yo[j], y_out[j])

                for e in range(HEAD):
                    expert(e, e)
                with act.Fori(0, TRIPS) as i:
                    for j in range(UNROLL):
                        expert(i * UNROLL + (HEAD + j), HEAD + j, i)
                for e in TAIL:
                    expert(e, e)
                n_over = act.value_load(over_i[0:1, OVER:OVER + 1], min_val=0, max_val=OVER)
                with act.If(n_over > 0):
                    all_rows_out(act, l)
                    with act.Fori(0, n_over) as o:
                        act.wait_ge(v_gu[l], o + 1)
                        act.activation(gated, ps[:, 1, :FH], ACT.Silu).then_inc(v_silu[l], 1)
                        act.wait_ge(v_y[l], o + 2)
                        act.activation(yo[0], ps[:, 2, :], ACT.Copy).then_inc(v_ya[l], 1)
                        act.wait_ge(v_ya[l], o + 1)
                        rows_to_dram(o * CAP + NE * CAP, yo[0], v_out[l])
                        act.wait_ge(v_out[l], o * 32 + 32)
                act.nop()

                def scale(i):
                    act.wait_ge(res_in[2 * q + i % 2], residual_target(q, i))
                    act.activation(res[i % 2], res[i % 2], ACT.Copy, scale=ALPHA).then_inc(scaled, 1)

                scale(0)
                scale(1)
                residual(q, 2)
                for t in range(NT):
                    if t + 3 < NT:
                        residual(q, t + 3)
                    if t + 2 < NT:
                        scale(t + 2)
                    act.wait_ge(x_done[q], t + 1)
                    rows = prompt_rows(t)
                    if l == 0:
                        act.dma_start(x2_dram[t * TT:(t + 1) * TT, :], zt(q, t)).then_inc(x_out(q, t), 16)
                        act.wait_ge(turned[1], t + 1)
                        act.activation(xT[:, :, t * TT:(t + 1) * TT],
                                       ps[:, 4:6, :4 * TT].rearrange("p a (k t) -> p a k t", k=4),
                                       ACT.Copy).then_inc(turned_sb[1], 1)
                    else:
                        act.dma_start(y_prompt[0, t * TT:t * TT + rows, :], zt(q, t)[:rows]).then_inc(x_out(q, t), 16)
                        if rows < TT:
                            act.dma_start(y_sample[:, 0, :], zt(q, t)[rows:]).then_inc(x_out(q, t), 16)
            all_out(act, 2 * DEPTH - 1)
            act.wait_ge(state_out, 16 * 8)

        @block.vector
        def _(dve):
            n = [0]

            def step(ins):
                n[0] += 1
                ins.then_inc(dve_c, 1)
                dve.wait_ge(dve_c, n[0])

            def tsc(out, x, s1, op, s2=None, op1=None):
                return dve.tensor_scalar(out, x, s1, s2, op, op1) if op1 else dve.tensor_scalar(out, x, s1, None, op)

            tt, stt = dve.tensor_tensor, dve.scalar_tensor_tensor

            for i in range(NT):
                dve.wait_ge(setup_mm, i + 1)
                dve.tensor_copy(xT[:, 0:4, i * TT:(i + 1) * TT],
                                ps[:, 2 * (i % 4), :4 * TT].rearrange("p (k t) -> p k t", k=4)).then_inc(setup_dve, 1)
            dve.wait_ge(setup_mm, NT + 1)
            dve.tensor_copy(feat[:, :, :], ps[:, 7, :KT * NROW].rearrange("p (c r) -> p c r", c=KT)
                            ).then_inc(setup_dve, 1)
            dve.wait_ge(setup_dve, NT + 1)

            lam = feat[:, :, R_LAM]
            step(tsc(spx[:, 3, :], lam, -1.0, ALU.mult))
            tt(spx[:, 1, :], spx[:, 3, :], lam, ALU.max).then_inc(lam_ok, 1)
            dve.wait_ge(lam_ok, 2)
            u, s, s2, y = spx[:, 2, :], spx[:, 4, :], spx[:, 5, :], spx[:, 0, :]
            step(tsc(s2, u, 2.0, ALU.add))
            step(dve.reciprocal(s, s2))
            step(tt(s, s, u, ALU.mult))
            step(tt(s2, s, s, ALU.mult))
            step(tsc(y, s2, 1.0 / 17, ALU.mult))
            for k in range(7, 0, -1):
                step(stt(y, y, 1.0 / (2 * k + 1), s2, ALU.add, ALU.mult))
            step(stt(y, y, 1.0, s, ALU.add, ALU.mult))
            step(tsc(s, spx[:, 3, :], 0.0, ALU.max))
            step(stt(y, y, 2.0, s, ALU.mult, ALU.add))
            tsc(y, y, -RG_C, ALU.mult).then_inc(lam_ok, 1)

            def state_taps(l, r_state, r_w, taps):
                out = conv0[:, l, :, :]
                for w in range(taps):
                    st = feat[:, :, r_state + w:r_state + DEC * taps:taps]
                    wv = feat[:, :, r_w + w:r_w + w + 1].broadcast_to([P, KT, DEC])
                    t = out if w == 0 else tmp[4][:, :KT * DEC].rearrange("p (c s) -> p c s", c=KT)
                    step(tt(t, st, wv, ALU.mult))
                    if w:
                        step(tt(out, out, t, ALU.add))
                if l == 1:
                    bv = feat[:, :, R_BB:R_BB + 1].broadcast_to([P, KT, DEC])
                    step(tt(out, out, bv, ALU.add))

            state_taps(0, R_SA, R_WA, WA - 1)
            state_taps(1, R_SB, R_WB, WB - 1)
            dve.memset(pad[:, :WA - 1], 0.0).then_inc(pad_ok, 1)
            dve.wait_ge(pad_ok, 1)

            def halves(v):
                return v.rearrange("p (a b) -> p a b", a=2)

            def banks(pair):
                return ps[:, 2 * pair:2 * pair + 2, :HALF]

            def tap(r, c):
                return feat[:, c, r:r + 1]

            for c in range(KT):
                dve.wait_ge(mm_in[0], 3 * c + 2)
                dve.wait_ge(ev_a[0], c + 1)
                u = pad[:, WA - 1:WA - 1 + T]
                tt(halves(u), banks((3 * c + 1) % 4), halves(tmp[c % 2]), ALU.mult).then_inc(ev_b[0], 1)
                dve.wait_ge(ev_b[0], c + 1)
                dve.tensor_copy(new_cols[:, c, :10], pad[:, SEQ:SEQ + 10])
                step(tsc(tmp[2][:, :SEQ], pad[:, :SEQ], tap(R_WA, c), ALU.mult))
                dve.tensor_copy(tmp[2][:, SEQ:], conv0[:, 0, c, :])
                step(stt(tmp[2][:, :SEQ], pad[:, 1:SEQ + 1], tap(R_WA + 1, c), tmp[2][:, :SEQ], ALU.mult, ALU.add))
                step(stt(tmp[3], u, tap(R_WA + 2, c), tmp[2], ALU.mult, ALU.add))
                dve.wait_ge(mm_in[0], 3 * c + 3)
                if c * T + T > 3 * D:
                    dve.wait_ge(zero_out, 16 * -(-OVER * CAP // P))
                tt(halves(hT[:, c, :]), banks((3 * c + 2) % 4), halves(tmp[3]), ALU.mult).then_inc(h_done[0], 1)

            def stats(q, i):
                z, st = zt(q, i), stat[:, i % 2, :]
                dve.wait_ge(z_done[q], i + 1)
                dve.bn_stats(st[:, 0:6], z[:, :512])
                step(dve.bn_stats(st[:, 6:12], z[:, 512:]))
                step(dve.bn_aggr(st[:, 12:14], st[:, 0:12]))
                tsc(st[:, 14:15], st[:, 13:14], LN_EPS, ALU.add).then_inc(var_ok[q], 1)

            def affine(q, i):
                z, st = zt(q, i), stat[:, i % 2, :]
                if i == 0:
                    dve.wait_ge(par_in, 32 * (q + 1))
                step(stt(z, z, st[:, 12:13], gain, ALU.subtract, ALU.mult))
                dve.wait_ge(rstd_ok[q], i + 1)
                stt(z, z, st[:, 15:16], shift, ALU.mult, ALU.add).then_inc(x_done[q], 1)

            for l in L:
                if l == 1:
                    R, I, DEC_A, TH, G1 = tmp[2], tmp[3], tmp[4], tmp[5], tmp[8]
                    dve.wait_ge(turned[1], NT)
                    all_out(dve, 1)
                    dve.memset(pad[:, :WB - 1], 0.0).then_inc(pad_ok, 1)

                    def conv(c):
                        x = tmp[6 + c % 2]
                        dve.wait_ge(ev_a[1], c + 1)
                        if c >= 2:
                            dve.wait_ge(h_done[1], c - 1)
                        dve.tensor_copy(new_cols[:, c, :11], pad[:, SEQ:SEQ + 11])
                        step(tsc(G1[:, :SEQ], pad[:, :SEQ], tap(R_WB, c), ALU.mult, tap(R_BB, c), ALU.add))
                        step(stt(G1[:, :SEQ], pad[:, 1:SEQ + 1], tap(R_WB + 1, c), G1[:, :SEQ], ALU.mult, ALU.add))
                        dve.tensor_copy(G1[:, SEQ:], conv0[:, 1, c, :])
                        step(stt(G1[:, :SEQ], pad[:, 2:SEQ + 2], tap(R_WB + 2, c), G1[:, :SEQ], ALU.mult, ALU.add))
                        stt(x, pad[:, WB - 1:], tap(R_WB + 3, c), G1, ALU.mult, ALU.add).then_inc(xc_done, 1)
                        dve.wait_ge(xc_done, c + 1)

                    def recurrence(c):
                        x, g = tmp[6 + c % 2], tmp[c % 2]
                        if c >= 1:
                            dve.wait_ge(h_done[1], c)
                        dve.wait_ge(ev_b[1], c + 1)
                        step(tt(G1, g, g, ALU.mult))
                        step(tsc(G1, G1, GELU_A, ALU.mult, 1.0, ALU.add))
                        tt(G1, G1, g, ALU.mult).then_inc(gelu_in, 1)
                        dve.wait_ge(sig_ok, 2 * c + 2)
                        step(tt(I, I, x, ALU.mult))
                        dve.wait_ge(decay_ok, 2 * c + 2)
                        step(stt(R, DEC_A, -1.0, DEC_A, ALU.mult, ALU.mult))
                        stt(R, R, -1.0, TH, ALU.add, ALU.mult).then_inc(sq_in, 1)
                        dve.wait_ge(gelu_ok, c + 1)
                        step(stt(G1, G1, 1.0, g, ALU.add, ALU.mult))
                        dve.wait_ge(sq_ok, c + 1)
                        step(tt(I, I, R, ALU.mult))
                        step(tt(TH[:, SEQ:], DEC_A[:, SEQ:], feat[:, c, R_H:R_H + DEC], ALU.mult))
                        step(tt(TH[:, SEQ:], TH[:, SEQ:], I[:, SEQ:], ALU.add))
                        step(dve.tensor_tensor_scan(TH[:, :SEQ], DEC_A[:, :SEQ], I[:, :SEQ], 0.0, ALU.mult, ALU.add))
                        dve.tensor_copy(new_cols[:, c, 11:20], TH[:, SEQ - 1:])
                        stt(hT[:, c, :], G1, 0.5, TH, ALU.mult, ALU.mult).then_inc(h_done[1], 1)

                    for c in range(KT):
                        conv(c)
                        if c >= 1:
                            recurrence(c - 1)
                    recurrence(KT - 1)

                q = 2 * l
                for i in range(NT):
                    if i >= 2:
                        dve.wait_ge(x_out(q, i), x_out_target(q, i - 2))
                        dve.wait_ge(turned[q], i - 1)
                    dve.wait_ge(res_in[2 * q + i % 2], residual_target(q, i))
                    dve.wait_ge(out_mm, NT * l + i + 1)
                    stt(zt(q, i).rearrange("r (a b) -> r a b", a=2), res[i % 2].rearrange("r (a b) -> r a b", a=2),
                        ALPHA, ps[:TT, 2 * (i % 2):2 * (i % 2) + 2, :], ALU.mult, ALU.add).then_inc(z_done[q], 1)
                    stats(q, i)
                    affine(q, i)

                dve.wait_ge(logit_mm, NT * (l + 1))
                dve.wait_ge(consts, 9)
                step(dve.tensor_copy(lg, ps[:TT, 6, :NT * (GROUPS + NE)].rearrange("p (i c) -> p i c", i=NT)))
                gl, el = lg[:, :, :GROUPS], lg[:, :, GROUPS:]

                def v5(k):
                    return s5[:, k, :]

                def over(v, n_):
                    return v.unsqueeze(2).broadcast_to([TT, NT, n_])

                def ranks(n_):
                    return rev[:, NE - n_:].unsqueeze(1).broadcast_to([TT, NT, n_])

                step(dve.tensor_reduce(v5(0), gl, AX, ALU.max))
                tt(gsh, gl, over(v5(0), GROUPS), ALU.subtract).then_inc(gsh_ok, 1)
                dve.wait_ge(gsh_ok, l + 1)
                step(tsc(ohg, gsh, 0.0, ALU.is_equal))
                step(tt(ohg, ohg, ranks(GROUPS), ALU.mult))
                step(dve.tensor_reduce(v5(1), ohg, AX, ALU.max))
                step(tt(ohg, over(v5(1), GROUPS), ranks(GROUPS), ALU.is_equal))
                dve.wait_ge(gex_ok, l + 1)
                step(dve.tensor_reduce(v5(2), gex, AX, ALU.add))
                step(dve.reciprocal(v5(3), v5(2)))
                step(tsc(ohg, ohg, BIG, ALU.mult, -BIG, ALU.add))
                for i in range(NT):
                    ins = tt(elm[:, i, :].rearrange("p (g e) -> p g e", g=GROUPS),
                             el[:, i, :].rearrange("p (g e) -> p g e", g=GROUPS),
                             ohg[:, i, :].unsqueeze(2).broadcast_to([TT, GROUPS, EPG]), ALU.add)
                step(ins)
                for k in range(TOPK):
                    step(dve.tensor_reduce(v5(4 + k), elm, AX, ALU.max))
                    step(tt(key, elm, over(v5(4 + k), NE), ALU.is_equal))
                    step(tt(key, key, ranks(NE), ALU.mult))
                    step(dve.tensor_reduce(s10[:, 0, k * NT:(k + 1) * NT], key, AX, ALU.max))
                    step(tt(oh[:, k], over(s10[:, 0, k * NT:(k + 1) * NT], NE), ranks(NE), ALU.is_equal))
                    if k == 0:
                        step(stt(elm, oh[:, k], -2.0 * BIG, elm, ALU.mult, ALU.add))
                tt(v5(7), v5(5), v5(4), ALU.subtract).then_inc(d_ok, 1)
                tt(picked[:, :, :], oh[:, 0], oh[:, 1], ALU.add).then_inc(pick_ok, 1)
                dve.wait_ge(e_ok, l + 1)
                step(tsc(v5(9), v5(8), 1.0, ALU.add))
                step(dve.reciprocal(v5(10), v5(9)))
                step(tt(wts[:, :NT], v5(3), v5(10), ALU.mult))
                step(tt(wts[:, NT:], wts[:, :NT], v5(8), ALU.mult))

                dve.wait_ge(rank_mm, l + 1)
                dve.tensor_copy(rank, ps[:TT, 7, :NT * NE].rearrange("p (i e) -> p i e", i=NT))
                step(dve.tensor_copy(cnt, ps[:TT, 7, NT * NE:(NT + 1) * NE]))
                step(tt(big8, cnt.unsqueeze(2).broadcast_to([TT, NE, MAXQ]),
                        thr[:, :].unsqueeze(1).broadcast_to([TT, NE, MAXQ]), ALU.is_gt))
                step(dve.tensor_reduce(nbl, big8, AX, ALU.add))
                step(dve.tensor_tensor_scan(cum, ones_f[:, :], nbl, 0.0, ALU.mult, ALU.add))
                step(tt(start, cum, nbl, ALU.subtract))

                def v10(k):
                    return s10[:, k, :]

                flat = rank.rearrange("p i e -> p (i e)").unsqueeze(1).broadcast_to([TT, TOPK, NT * NE])
                step(tt(prod, oh.rearrange("p k i e -> p k (i e)"), flat, ALU.mult))
                step(dve.tensor_reduce(v10(1), prod.rearrange("p k (i e) -> p (k i) e", e=NE), AX, ALU.add))
                ohv = oh.rearrange("p k i e -> p (k i) e")
                pv = prod.rearrange("p k (i e) -> p (k i) e", e=NE)
                step(tt(pv, ohv, start.unsqueeze(1).broadcast_to([TT, TOPK * NT, NE]), ALU.mult))
                step(dve.tensor_reduce(v10(2), pv, AX, ALU.add))
                step(tt(cmpq, v10(1).unsqueeze(2).broadcast_to([TT, TOPK * NT, MAXQ]),
                        thr[:, :].unsqueeze(1).broadcast_to([TT, TOPK * NT, MAXQ]), ALU.is_ge))
                step(dve.tensor_reduce(v10(3), cmpq, AX, ALU.add))
                step(stt(v10(4), v10(3), -float(CAP), v10(1), ALU.mult, ALU.add))
                step(tsc(v10(5), v10(0), -1.0, ALU.mult, float(NE), ALU.add))
                step(tsc(v10(6), v10(3), 1.0, ALU.is_ge))
                step(stt(v10(7), v10(2), float(NE - 1), v10(3), ALU.add, ALU.add))
                step(tt(v10(7), v10(7), v10(5), ALU.subtract))
                step(tt(v10(7), v10(7), v10(6), ALU.mult))
                step(tt(v10(7), v10(7), v10(5), ALU.add))
                step(stt(slot_i[:, :], v10(7), float(CAP), v10(4), ALU.mult, ALU.add))
                step(tt(rowhot, v10(4).unsqueeze(2).broadcast_to([TT, TOPK * NT, CAP]),
                        iota[:, :CAP].unsqueeze(1).broadcast_to([TT, TOPK * NT, CAP]), ALU.is_equal))
                step(tt(blkhot, v10(7).unsqueeze(2).broadcast_to([TT, TOPK * NT, NBLK]),
                        iota[:, :NBLK].unsqueeze(1).broadcast_to([TT, TOPK * NT, NBLK]), ALU.is_equal))
                for k in range(TOPK):
                    b = blkhot[:, k * NT:(k + 1) * NT, :]
                    ins = tt(b, b, over(tokid[:, :], NBLK), ALU.mult)
                ins.then_inc(hot_ok, 1)
                dve.wait_ge(idx_mm, l + 1)
                dve.tensor_copy(idx[:, :], ps[:CAP, 5, :NBLK]).then_inc(idx_ok[l], 1)
                step(tt(ovcmp, cum[0:1, :].unsqueeze(1).broadcast_to([1, OVER, NE]),
                        iota[0:1, :OVER].unsqueeze(2).broadcast_to([1, OVER, NE]), ALU.is_le))
                step(dve.tensor_reduce(s10[0:1, 8:12, :].rearrange("p a b -> p (a b)")[:, :OVER], ovcmp, AX, ALU.add))
                dve.tensor_copy(over_i[:, OVER:], cum[0:1, NE - 1:])
                tsc(over_i[:, :OVER], s10[0:1, 8:12, :].rearrange("p a b -> p (a b)")[:, :OVER], float(NE - 1),
                    ALU.min).then_inc(idx_ok[l], 1)

                def turned_rows(done, ready, v):
                    dve.wait_ge(done, v)
                    dve.tensor_copy(xgT, ps[:, 0, :KT * ROWS].rearrange("p (k t) -> p k t", k=KT)).then_inc(ready, 1)

                def hidden(ready):
                    tt(h, gated, ps[:, 1, FH:2 * FH], ALU.mult).then_inc(ready, 1)

                def turned_hidden(ready):
                    dve.tensor_copy(hidT, ps[:, 4, :FT * ROWS]).then_inc(ready, 1)

                def expert(e, more=True):
                    dve.wait_ge(silu_ok[l], e + 1)
                    hidden(hid_ok[l])
                    if more:
                        turned_rows(t_mm[l], t_sb[l], e + 2)
                    dve.wait_ge(h_mm[l], e + 1)
                    dve.wait_ge(y_mm[l], e)
                    turned_hidden(h_sb[l])

                turned_rows(t_mm[l], t_sb[l], 1)
                for e in range(HEAD):
                    expert(e)
                with dve.Fori(0, TRIPS) as i:
                    for j in range(UNROLL):
                        expert(i * UNROLL + (HEAD + j))
                for e in TAIL:
                    expert(e, more=(e < NE - 1))
                n_over = dve.value_load(over_i[0:1, OVER:OVER + 1], min_val=0, max_val=OVER)
                with dve.If(n_over > 0):
                    dve.wait_ge(y_mm[l], NE)
                    with dve.Fori(0, n_over) as o:
                        turned_rows(v_tmm[l], v_tsb[l], o + 1)
                        dve.wait_ge(v_silu[l], o + 1)
                        hidden(v_hid[l])
                        dve.wait_ge(v_hmm[l], o + 1)
                        turned_hidden(v_hsb[l])
                        dve.wait_ge(v_out[l], o * 32 + 32)
                    dve.memset(s5[:, 15, :], 0.0).then_inc(over_done[l], 1)
                dve.nop()

                q = 2 * l + 1
                for i in range(NT + 1):
                    if i < NT:
                        z = zt(q, i)
                        dve.wait_ge(pick_in[2 * l + i % 2], 32 * (i // 2 + 1))
                        dve.wait_ge(scaled, NT * l + i + 1)
                        step(stt(z, z, wts[:, i:i + 1], res[i % 2], ALU.mult, ALU.add))
                        stt(z, r2[i % 2], wts[:, NT + i:NT + i + 1], z, ALU.mult, ALU.add).then_inc(z_done[q], 1)
                        stats(q, i)
                    if i >= 1:
                        affine(q, i - 1)


_OUTS = [(1, SEQ, D), (DEC, 1, D), (1, 1, WA - 1, D), (1, DEC, WA - 1, D), (1, 1, WB - 1, D),
         (1, DEC, WB - 1, D), (1, 1, D), (1, DEC, D)]


def kernel(**inputs):
    import numpy as np
    import concourse.bacc as bacc
    from concourse.bass_utils import run_bass_kernel_spmd

    nc = bacc.Bacc("TRN2", target_bir_lowering=False, num_devices=1)
    arrays, args = {}, {}
    for name in inputs:
        x = np.ascontiguousarray(inputs[name])
        arrays[f"in_{name}"] = x
        args[name] = nc.dram_tensor(f"in_{name}", x.shape, mybir.dt.from_np(x.dtype), kind="ExternalInput").ap()
    outs = [nc.dram_tensor(f"out_{i}", list(s), F32, kind="ExternalOutput").ap() for i, s in enumerate(_OUTS)]
    build(nc, args, outs)
    r = run_bass_kernel_spmd(nc, [arrays], core_ids=[0])
    return tuple(r.results[0][f"out_{i}"] for i in range(len(_OUTS)))
```
